# Optimizing a Trainium2 kernel written in Bass

```python
import math
import jax
import jax.numpy as jnp
from jax import lax
import numpy as np

D_MODEL = 1024
BATCH = 1
SEQ = 256
DEPTH = 1

NORM_EPS = 1e-5

ATT_HEAD_DIM = 128
ATT_HEADS_PER_GROUP = 4
DILATED_GROUPS = ((128, 1), (512, 4), (2048, 16))
N_ATT_GROUPS = len(DILATED_GROUPS)
N_ATT_HEADS = N_ATT_GROUPS * ATT_HEADS_PER_GROUP
ATT_OUT_WIDTH = ATT_HEADS_PER_GROUP * ATT_HEAD_DIM
REL_BUCKETS = 32
REL_MAX_DIST = 2048

RET_HEADS = 4
RET_DK = 128
RET_DV = 256
RET_CHUNK = 128
ROPE_BASE = 10000.0

PROJ_SPLITS = (
    N_ATT_HEADS * ATT_HEAD_DIM, N_ATT_HEADS * ATT_HEAD_DIM, N_ATT_HEADS * ATT_HEAD_DIM,
    RET_HEADS * RET_DK, RET_HEADS * RET_DK,
    RET_HEADS * RET_DV, RET_HEADS * RET_DV,
    D_MODEL, D_MODEL,
)
PROJ_WIDTH = sum(PROJ_SPLITS)
PROJ_OFFSETS = tuple(int(v) for v in np.cumsum(PROJ_SPLITS)[:-1])

N_EXPERTS = 32
TOP_K = 4
D_EXPERT = 1024
SWIGLU_LIMIT = 7.0
SWIGLU_ALPHA = 1.702
MOE_BLOCK = 256

kernel_name = "hybrid_dilated_retention_moe_block"

def rmsnorm(x, g):
    xf = x.astype(jnp.float32)
    y = xf * lax.rsqrt(jnp.mean(xf * xf, axis=-1, keepdims=True) + NORM_EPS)
    return (y * g.astype(jnp.float32)).astype(x.dtype)

def t5_bucket(dist):
    max_exact = REL_BUCKETS // 2
    d_f = jnp.maximum(dist, 1).astype(jnp.float32)
    large = max_exact + (jnp.log(d_f / max_exact) / math.log(REL_MAX_DIST / max_exact)
                         * (REL_BUCKETS - max_exact)).astype(jnp.int32)
    large = jnp.minimum(large, REL_BUCKETS - 1)
    return jnp.where(dist < max_exact, dist, large)

def dilated_window_attention(q, k, v, rel_bias, dilation, n_steps):
    B, S, H, E = q.shape
    L = S // dilation
    nb = -(-L // n_steps)
    Lp = nb * n_steps

    def to_blocks(t):
        t = t.reshape(B, L, dilation, H, E).transpose(0, 2, 1, 3, 4)
        t = jnp.pad(t, ((0, 0), (0, 0), (0, Lp - L), (0, 0), (0, 0)))
        return t.reshape(B, dilation, nb, n_steps, H, E)

    def with_prev(t):
        prev = jnp.pad(t, ((0, 0), (0, 0), (1, 0), (0, 0), (0, 0), (0, 0)))[:, :, :-1]
        return jnp.concatenate([prev, t], axis=3)

    qb = to_blocks(q)
    kw = with_prev(to_blocks(k))
    vw = with_prev(to_blocks(v))

    qi = jnp.arange(n_steps)[:, None]
    kj = jnp.arange(2 * n_steps)[None, :]
    step_dist = qi + n_steps - kj
    band = (step_dist >= 0) & (step_dist <= n_steps)
    key_step = jnp.arange(nb)[:, None] * n_steps + kj - n_steps
    valid = band[None] & (key_step >= 0)[:, None, :]
    bias = rel_bias[t5_bucket(jnp.maximum(step_dist, 0) * dilation)]
    bias = bias.astype(jnp.float32).transpose(2, 0, 1)

    scale = E ** -0.5
    logits = jnp.einsum('brnqhe,brnkhe->brnhqk', qb, kw).astype(jnp.float32) * scale + bias
    logits = jnp.where(valid[None, None, :, None], logits, -jnp.inf)
    m = jnp.max(logits, axis=-1, keepdims=True)
    p = jnp.exp(logits - m)
    denom = jnp.sum(p, axis=-1)
    o = jnp.einsum('brnhqk,brnkhe->brnqhe', p, vw.astype(jnp.float32))
    o = o / denom.transpose(0, 1, 2, 4, 3)[..., None]
    lse = (m[..., 0] + jnp.log(denom)).transpose(0, 1, 2, 4, 3)

    o = o.reshape(B, dilation, Lp, H, E)[:, :, :L].transpose(0, 2, 1, 3, 4).reshape(B, S, H, E)
    lse = lse.reshape(B, dilation, Lp, H)[:, :, :L].transpose(0, 2, 1, 3).reshape(B, S, H)
    return o, lse

def rotary(t):
    S, E = t.shape[1], t.shape[-1]
    inv = ROPE_BASE ** (-jnp.arange(0, E, 2, dtype=jnp.float32) / E)
    ang = jnp.arange(S, dtype=jnp.float32)[:, None] * inv[None]
    cos = jnp.cos(ang)[None, :, None, :]
    sin = jnp.sin(ang)[None, :, None, :]
    tf = t.astype(jnp.float32)
    t1, t2 = tf[..., 0::2], tf[..., 1::2]
    return jnp.stack([t1 * cos - t2 * sin, t1 * sin + t2 * cos], axis=-1).reshape(t.shape)

def retention_chunkwise(q, k, v):
    B, S, H, dk = q.shape
    dv = v.shape[-1]
    C = RET_CHUNK
    nc = S // C
    log_g = jnp.log(1.0 - 2.0 ** (-5.0 - jnp.arange(H, dtype=jnp.float32)))
    idx = jnp.arange(C, dtype=jnp.float32)
    diff = idx[:, None] - idx[None, :]
    decay = jnp.where(diff >= 0, jnp.exp(jnp.maximum(diff, 0.0)[None] * log_g[:, None, None]), 0.0)
    xi = jnp.exp((idx + 1.0)[:, None] * log_g[None])
    zeta = jnp.exp((C - 1.0 - idx)[:, None] * log_g[None])
    g_chunk = jnp.exp(C * log_g)

    qc = q.reshape(B, nc, C, H, dk)
    kc = k.reshape(B, nc, C, H, dk)
    vc = v.reshape(B, nc, C, H, dv)
    scores = jnp.einsum('bnihd,bnjhd->bnhij', qc, kc) * decay
    inner = jnp.einsum('bnhij,bnjhe->bnihe', scores, vc)

    def step(R, xs):
        q_n, k_n, v_n = xs
        cross = jnp.einsum('bihd,bhde->bihe', q_n, R) * xi[None, :, :, None]
        R = R * g_chunk[None, :, None, None] + jnp.einsum('bjhd,bjhe->bhde', k_n * zeta[None, :, :, None], v_n)
        return R, cross

    R0 = jnp.zeros((B, H, dk, dv), jnp.float32)
    _, cross = lax.scan(step, R0, (qc.transpose(1, 0, 2, 3, 4), kc.transpose(1, 0, 2, 3, 4),
                                   vc.transpose(1, 0, 2, 3, 4)))
    cross = cross.transpose(1, 0, 2, 3, 4)
    return (inner + cross).reshape(B, S, H, dv)

def moe_ffn(h, w_router, b_router, w1, b1, w2, b2):
    B, S, D = h.shape
    T = B * S
    M = MOE_BLOCK
    F = D_EXPERT
    xt = h.reshape(T, D)
    logits = (xt @ w_router + b_router).astype(jnp.float32)
    top_vals, top_idx = lax.top_k(logits, TOP_K)
    gates = jax.nn.softmax(top_vals, axis=-1)

    A = T * TOP_K
    e_flat = top_idx.reshape(A)
    tok_flat = jnp.broadcast_to(jnp.arange(T, dtype=jnp.int32)[:, None], (T, TOP_K)).reshape(A)
    w_flat = gates.reshape(A)
    order = jnp.argsort(e_flat)
    e_sorted = e_flat[order]
    tok_sorted = tok_flat[order]
    w_sorted = w_flat[order]

    counts = jnp.bincount(e_flat, length=N_EXPERTS)
    padded = ((counts + M - 1) // M) * M
    start = jnp.cumsum(counts) - counts
    pend = jnp.cumsum(padded)
    pstart = pend - padded
    pos = pstart[e_sorted] + jnp.arange(A) - start[e_sorted]
    nblk = -(-A // M) + N_EXPERTS
    P = nblk * M
    buf_tok = jnp.full((P,), T, jnp.int32).at[pos].set(tok_sorted)
    buf_w = jnp.zeros((P,), jnp.float32).at[pos].set(w_sorted)
    blk_expert = jnp.minimum(jnp.searchsorted(pend, jnp.arange(nblk) * M, side='right'), N_EXPERTS - 1)

    x_pad = jnp.concatenate([xt, jnp.zeros((1, D), xt.dtype)], axis=0)

    def expert_block(args):
        tok, e = args
        xb = x_pad[tok]
        gu = xb @ w1[e] + b1[e]
        gate = jnp.minimum(gu[:, :F], SWIGLU_LIMIT)
        up = jnp.clip(gu[:, F:], -SWIGLU_LIMIT, SWIGLU_LIMIT)
        act = (up + 1.0) * gate * jax.nn.sigmoid(SWIGLU_ALPHA * gate)
        return act @ w2[e] + b2[e]

    yb = lax.map(expert_block, (buf_tok.reshape(nblk, M), blk_expert))
    y = yb.reshape(P, D) * buf_w[:, None].astype(yb.dtype)
    out = jnp.zeros((T + 1, D), yb.dtype).at[buf_tok].add(y)[:T]
    return out.reshape(B, S, D).astype(h.dtype)

def setup_inputs(seed: int = 0) -> dict:
    key = jax.random.key(seed)
    ks = jax.random.split(key, 16)
    D = D_MODEL
    nrm = jax.random.normal
    ret_w = RET_HEADS * RET_DV
    return {
        "x": nrm(ks[0], (BATCH, SEQ, D), jnp.float32),
        "norm_mix_g": 1.0 + 0.02 * nrm(ks[1], (DEPTH, D), jnp.float32),
        "w_in": nrm(ks[2], (DEPTH, D, PROJ_WIDTH), jnp.float32) * D ** -0.5,
        "rel_bias": 0.5 * nrm(ks[3], (REL_BUCKETS, N_ATT_HEADS), jnp.float32),
        "w_att_branch": nrm(ks[4], (DEPTH, ATT_OUT_WIDTH, D), jnp.float32) * ATT_OUT_WIDTH ** -0.5,
        "w_ret_branch": nrm(ks[5], (DEPTH, ret_w, D), jnp.float32) * ret_w ** -0.5,
        "w_out": nrm(ks[6], (DEPTH, D, D), jnp.float32) * D ** -0.5,
        "norm_ffn_g": 1.0 + 0.02 * nrm(ks[7], (DEPTH, D), jnp.float32),
        "w_router": nrm(ks[8], (DEPTH, D, N_EXPERTS), jnp.float32) * D ** -0.5,
        "b_router": 0.01 * nrm(ks[9], (DEPTH, N_EXPERTS), jnp.float32),
        "w1": nrm(ks[10], (DEPTH, N_EXPERTS, D, 2 * D_EXPERT), jnp.float32) * D ** -0.5,
        "b1": 0.01 * nrm(ks[11], (DEPTH, N_EXPERTS, 2 * D_EXPERT), jnp.float32),
        "w2": nrm(ks[12], (DEPTH, N_EXPERTS, D_EXPERT, D), jnp.float32) * D_EXPERT ** -0.5,
        "b2": 0.01 * nrm(ks[13], (DEPTH, N_EXPERTS, D), jnp.float32),
        "norm_final_g": 1.0 + 0.02 * nrm(ks[14], (D,), jnp.float32),
    }

def reference(x, norm_mix_g, w_in, rel_bias, w_att_branch, w_ret_branch, w_out, norm_ffn_g,
              w_router, b_router, w1, b1, w2, b2, norm_final_g):
    B, S, D = x.shape
    for layer in range(DEPTH):
        h = rmsnorm(x, norm_mix_g[layer])
        proj = h @ w_in[layer]
        q_a, k_a, v_a, q_r, k_r, v_r, g_r, gate_a, gate_r = jnp.split(proj, PROJ_OFFSETS, axis=-1)

        q_a = q_a.reshape(B, S, N_ATT_HEADS, ATT_HEAD_DIM)
        k_a = k_a.reshape(B, S, N_ATT_HEADS, ATT_HEAD_DIM)
        v_a = v_a.reshape(B, S, N_ATT_HEADS, ATT_HEAD_DIM)
        outs, lses = [], []
        for g, (window, dilation) in enumerate(DILATED_GROUPS):
            hs = slice(g * ATT_HEADS_PER_GROUP, (g + 1) * ATT_HEADS_PER_GROUP)
            o_g, lse_g = dilated_window_attention(q_a[:, :, hs], k_a[:, :, hs], v_a[:, :, hs],
                                                  rel_bias[:, hs], dilation, window // dilation)
            outs.append(o_g)
            lses.append(lse_g)
        wts = jax.nn.softmax(jnp.stack(lses, axis=0), axis=0)
        att = jnp.sum(wts[..., None] * jnp.stack(outs, axis=0), axis=0)
        att = att.reshape(B, S, ATT_OUT_WIDTH).astype(x.dtype)

        q_r = rotary(q_r.reshape(B, S, RET_HEADS, RET_DK))
        k_r = rotary(k_r.reshape(B, S, RET_HEADS, RET_DK)) * RET_DK ** -0.5
        v_r = v_r.reshape(B, S, RET_HEADS, RET_DV).astype(jnp.float32)
        ret = retention_chunkwise(q_r, k_r, v_r)
        mu = jnp.mean(ret, axis=-1, keepdims=True)
        var = jnp.mean(jnp.square(ret - mu), axis=-1, keepdims=True)
        ret = (ret - mu) * lax.rsqrt(var + NORM_EPS)
        ret = (jax.nn.silu(g_r.astype(jnp.float32)) * ret.reshape(B, S, RET_HEADS * RET_DV)).astype(x.dtype)

        merged = (jax.nn.sigmoid(gate_a) * (att @ w_att_branch[layer])
                  + jax.nn.sigmoid(gate_r) * (ret @ w_ret_branch[layer]))
        x = x + merged @ w_out[layer]

        hf = rmsnorm(x, norm_ffn_g[layer])
        x = x + moe_ffn(hf, w_router[layer], b_router[layer], w1[layer], b1[layer], w2[layer], b2[layer])
    return rmsnorm(x, norm_final_g)


_drawn_inputs = setup_inputs


def setup_inputs(seed=0):
    import zlib

    import numpy as np

    out = dict(_drawn_inputs(seed))
    spreads = {}
    factors = {'b1': 8.0, 'b2': 8.0, 'norm_final_g': 2.874}
    for name, (base, spread) in spreads.items():
        noise = np.random.default_rng([zlib.crc32(name.encode()), seed]).standard_normal(out[name].shape)
        drawn = base * np.exp(spread * noise) if base else spread * noise
        out[name] = jnp.asarray(drawn.astype(out[name].dtype))
    for name, factor in factors.items():
        out[name] = (out[name] * factor).astype(out[name].dtype)
    return out
```

```python
from contextlib import ExitStack

import numpy as np

import concourse.bass as bass
from concourse import mybir

ALU = mybir.AluOpType
ACT = mybir.ActivationFunctionType
AX = mybir.AxisListType
F32 = mybir.dt.float32
BF16 = mybir.dt.bfloat16
I32 = mybir.dt.int32
U32 = mybir.dt.uint32

P = 128
D = 1024
T = 256
KC = D // P
TT = T // P
EPS = 1e-5
HALF = 512

SLOTS = 4
GROUPS = 3
N_ATT_HEADS = SLOTS * GROUPS
WINDOWS = ((128, 1), (512, 4), (2048, 16))
ATT_SCALE = 128.0 ** -0.5
REL_BUCKETS, REL_MAX_DIST = 32, 2048
MASKED = -1.0e30
RH = 4
DV = 256

N_EXP = 32
TOP_K = 4
F = 1024
CAP = 64
FQ = F // P
LIMIT = 7.0
ALPHA = 1.702
MAX_EXTRA = 16

GROUP_COLS = [0, 512, 1024, 1536, 2048, 2560, 4608, 5120,
              3072, 3584, 4096, 5632, 6144, 6656, 7168,
              7680, 8192, 8704, 9216]
N_GROUPS = len(GROUP_COLS)
QK_GROUPS = 8
W_BUFS = 4


def host_constants():
    f = np.float32
    p = np.arange(P)
    t = np.arange(T)
    ident = np.eye(P, dtype=f)
    rot = np.zeros((P, P), f)
    rot[p[1::2], p[0::2]] = -1.0
    rot[p[0::2], p[1::2]] = 1.0
    inv = (f(10000.0) ** (-np.arange(0, P, 2, dtype=f) / f(P))).astype(f)
    ang = (t.astype(f)[:, None] * inv[None]).astype(f)
    cos = np.repeat(np.cos(ang).T, 2, axis=0).astype(f)
    sin = np.repeat(np.sin(ang).T, 2, axis=0).astype(f)
    log_g = np.log(1.0 - 2.0 ** (-5.0 - np.arange(RH)))
    dist = t[None, :] - p[:, None]
    decay = np.where(dist[:, None] >= 0, np.exp(np.maximum(dist, 0)[:, None] * log_g[None, :, None]), 0.0)
    decay = (decay * P ** -0.5).astype(f).reshape(P, RH * T)
    before = (p[:, None] < p[None, :]).astype(f)
    ones = np.ones((P, P), f)
    slot = np.tile(np.arange(CAP, dtype=f), (P, 2))
    first_row = np.zeros((P, CAP), f)
    first_row[0] = 1.0
    early = np.concatenate([rot, cos, sin, ident[::-1]], axis=1)
    lasting = np.concatenate([ident, before, ones, slot, first_row], axis=1)
    d = 255 - np.arange(384)
    exact = REL_BUCKETS // 2
    large = exact + (np.log(np.maximum(d, 1).astype(f) / f(exact)) / f(np.log(REL_MAX_DIST / exact))
                     * f(REL_BUCKETS - exact)).astype(np.int32)
    bucket = np.where(d < exact, np.maximum(d, 0), np.minimum(large, REL_BUCKETS - 1))
    onehot = (np.arange(REL_BUCKETS)[:, None] == bucket[None]).astype(f)
    mask = np.zeros((N_ATT_HEADS, 384), f)
    for g, (window, dilation) in enumerate(WINDOWS):
        seen = (d >= 0) & (d % dilation == 0) & (d <= window)
        mask[g * SLOTS:(g + 1) * SLOTS] = np.where(seen, 0.0, MASKED)
    item = np.tile((P - np.arange(P, dtype=f)), (1, 1))
    e_of = np.tile(np.arange(N_EXP, dtype=f), (P, 1))
    return {"c_early": early, "c_lasting": lasting, "c_decay": decay, "c_onehot": onehot,
            "c_mask": mask, "c_item": item, "c_expert": e_of}


def hybrid_block_kernel(nc, x_in, g_mix, w_in, rel_bias, w_att, w_ret, w_out, g_ffn, w_router, b_router,
                        w1, b1, w2, b2, g_final, c_early, c_lasting, c_decay, c_onehot, c_mask, c_item,
                        c_expert, out):
    with ExitStack() as ctx:
        def sb(name, shape, dt=F32):
            return ctx.enter_context(nc.sbuf_tensor(name, shape, dt))

        def sem(name):
            return ctx.enter_context(nc.semaphore(name))

        ps = ctx.enter_context(nc.psum_tensor("ps", [P, 8, HALF], F32))
        psf = ps[:, :, :].rearrange("p b n -> p (b n)")

        def bank(b, n=1):
            return psf[:, b * HALF:(b + n) * HALF]

        w1_ring = sb("w1_ring", [P, KC, 2 * F])
        w2_ring = sb("w2_ring", [P, FQ, D])
        w1_flat = w1_ring[:, :, :].rearrange("p k n -> p (k n)")
        w2_flat = w2_ring[:, :, :].rearrange("p k n -> p (k n)")
        win = [w1_flat[:, b * KC * HALF:(b + 1) * KC * HALF].rearrange("p (k n) -> p k n", k=KC)
               for b in range(W_BUFS)]

        xb = sb("xb", [P, TT, D])
        A_QK = sb("A_QK", [P, 8192 + 2048])
        A_W = sb("A_W", [P, 8192])
        A_PT = sb("A_PT", [P, 2304])
        gr = sb("gr", [P, TT, D])
        attT = sb("attT", [P, SLOTS, T])
        gain = sb("gain", [P, D])
        lasting = sb("lasting", [P, 4 * P + CAP])
        before_bf = sb("before_bf", [P, P], BF16)
        ones_bf = sb("ones_bf", [P, P], BF16)
        wr_sb = sb("wr_sb", [P, KC, N_EXP])
        br_sb = sb("br_sb", [P, N_EXP])
        item_sb = sb("item_sb", [1, P])
        expert_sb = sb("expert_sb", [P, N_EXP])
        small = sb("small", [P, 192])
        ident = lasting[:, 0:P]
        slot_ids = lasting[:, 3 * P:4 * P]
        first_row = lasting[:, 4 * P:4 * P + CAP]

        qk = A_QK[:, 0:8192].rearrange("p (g c t) -> p g c t", g=QK_GROUPS, c=4)
        early = A_QK[:, 8192:8192 + 768]
        rot, cosT, sinT, flip = early[:, 0:P], early[:, P:P + T], early[:, P + T:P + 2 * T], early[:, P + 2 * T:2 * P + 2 * T]
        gateA = A_QK[:, 0:2048].rearrange("p (c t) -> p c t", c=KC)
        gateR = A_QK[:, 2048:4096].rearrange("p (c t) -> p c t", c=KC)
        retT = A_QK[:, 4096:6144].rearrange("p (c t) -> p c t", c=KC)
        watt = A_QK[:, 6144:10240].rearrange("p (c n) -> p c n", c=4)
        vA = A_W[:, 0:3072].rearrange("p (t n) -> p t n", t=TT)
        vR = A_W[:, 3072:5120].rearrange("p (t n) -> p t n", t=TT)
        hT = A_W[:, 5120:7168].rearrange("p (k t) -> p k t", k=KC)
        wout = A_W[:, 0:8192].rearrange("p (k n) -> p k n", k=KC)
        rel_sb = A_W[0:REL_BUCKETS, 7168:7168 + N_ATT_HEADS]
        onehot_sb = A_W[0:REL_BUCKETS, 7200:7584]
        mask_sb = A_W[0:N_ATT_HEADS, 7584:7968]
        tab_sb = w2_flat[0:N_ATT_HEADS, 7168:7552]
        toep_up = w2_flat[:, 4096:7168]
        ptb = A_PT[:, 0:2304].rearrange("p (b g q) -> p b g q", b=2, g=GROUPS)
        mergedT = A_PT[:, 0:2048].rearrange("p (c t) -> p c t", c=KC)
        toep = w2_flat[:, 0:3072].rearrange("p (h c) -> p h c", h=N_ATT_HEADS)
        decay = w2_flat[:, 3072:4096].rearrange("p (h i) -> p h i", h=RH)
        probs = w2_flat[:, 4096:6400].rearrange("p (b g k) -> p b g k", b=2, g=GROUPS)
        st = w2_flat[:, 6400:7936].rearrange("p (h i) -> p h i", h=RH)
        rtmp = w2_flat[:, 4096:5120]
        diag = gr[:, 1, :].rearrange("p (b q) -> p b q", b=8)
        wret = w2_flat.rearrange("p (k n) -> p k n", k=KC)

        xn = A_QK[:, 0:2048].rearrange("p (t d) -> p t d", t=TT)
        xnT = A_QK[:, 2048:4096].rearrange("p (k t) -> p k t", k=KC)
        xs = A_QK[:, 4096:7168].bitcast(BF16).rearrange("p (s t d) -> p s t d", s=3, t=TT)
        junk = A_QK[:, 7168:8192]
        posm = A_QK[:, 8192:8448].rearrange("p (t c) -> p t c", t=TT)
        gates = A_QK[:, 8448:8704].rearrange("p (t c) -> p t c", t=TT)
        top = A_QK[:, 8704:8960]
        b1_row = A_W[:, 0:2048]
        XT = A_W[:, 2048:2560].rearrange("p (k s) -> p k s", k=KC)
        gl = A_W[:, 2560:3072]
        ul = A_W[:, 3072:3584]
        sg = A_W[:, 3584:4096]
        act_sb = A_W[:, 4096:4608]
        actT = A_W[:, 4608:5120]
        y_sb = A_W[:, 5120:5632]
        sc_w = A_W[:, 5632:6144].rearrange("p (c t) -> p c t", c=2)
        s_w = A_W[:, 6144:6400].rearrange("p (t s) -> p t s", t=TT)
        s_one = A_W[:, 6400:6464].bitcast(BF16).rearrange("p (t s) -> p t s", t=TT)
        b2_sb = A_W[0:N_EXP, 6464:7488]
        gT = A_W[0:N_EXP, 7488:7744]
        lists = A_W[0:1, 7744:7872]
        list_i = lists.bitcast(I32)
        mask_f = A_W[:, 4608:4672].rearrange("p (t e) -> p t e", t=TT)
        mask_bf = sb("mask_bf", [P, TT, N_EXP], BF16)

        scratch = nc.dram_tensor("bias_scratch", (N_ATT_HEADS, 384), F32, kind="Internal").ap()

        ssq, rstd = small[:, 0:2], small[:, 2:4]
        negmax = small[:, 8:16]
        denom = small[:, 16:24]
        rden = small[:, 24:32]
        bns = small[:, 32:80].rearrange("p (g s) -> p g s", g=8)
        mv = small[:, 80:96].rearrange("p (g s) -> p g s", g=8)
        rrstd = small[:, 96:104]
        maxes = small[:, 104:112]

        s_x = [sem(f"x_loaded{t}") for t in range(TT)]
        s_gain = sem("gain_loaded")
        s_early = sem("early_tables_loaded")
        s_last = sem("lasting_tables_loaded")
        s_biasin = sem("bias_tables_loaded")
        s_small = sem("router_loaded")
        s_decay = sem("decay_loaded")
        s_tab = sem("bias_table_stored")
        s_toep = sem("bias_tiles_loaded")
        s_flip = sem("bias_tiles_turned")
        s_flipe = sem("bias_tiles_stored")
        s_win = [sem(f"w_in_loaded{b}") for b in range(W_BUFS)]
        s_watt = sem("w_att_loaded")
        s_wret = sem("w_ret_loaded")
        s_wouta = sem("w_out_head_loaded")
        s_woutb = sem("w_out_tail_loaded")
        s_b2 = sem("b2_loaded")
        s_out = sem("out_stored")

        s_dve = sem("vector_steps")
        s_sq = sem("squares_summed")
        s_root = sem("roots_done")
        s_ms = sem("mean_squares")
        s_h = sem("normed")
        s_ht = sem("normed_transposed")
        s_hte = sem("normed_transposed_stored")
        s_tabp = sem("bias_table_multiplied")
        s_tabd = sem("bias_table_ready")
        s_proj = sem("projection_done")
        s_proje = sem("projection_stored")
        s_rotm = sem("rotated_pairs")
        s_rotd = sem("rotary_done")
        s_sc = sem("scores_done")
        s_sce = sem("scores_stored")
        s_max = sem("maxima_ready")
        s_exp = sem("exps_done")
        s_diag = sem("diag_ready")
        s_pt = sem("probs_transposed")
        s_pte = sem("probs_transposed_stored")
        s_pv = sem("att_done")
        s_pve = sem("att_stored")
        s_rs = sem("ret_scores_done")
        s_rse = sem("ret_scores_stored")
        s_ro = sem("ret_out_done")
        s_rv = sem("ret_variances_ready")
        s_rr = sem("ret_roots_done")
        s_rg = sem("ret_gated")
        s_rt = sem("ret_transposed")
        s_rte = sem("ret_transposed_stored")
        s_br = sem("branches_done")
        s_mg = sem("merged_ready")
        s_wo = sem("w_out_done")
        s_x2 = sem("residual_ready")
        s_xt = sem("xn_transposed")
        s_xte = sem("xn_transposed_stored")
        s_lg = sem("logits_done")
        s_tk = sem("top_values_ready")
        s_tke = sem("gate_exps_done")
        s_mask = sem("routing_masks_ready")
        s_pos = sem("positions_done")
        s_table = sem("routing_tables_ready")
        s_gtp = sem("gates_transposed")
        s_gte = sem("gates_transposed_stored")
        s_bias2 = sem("b2_added")
        s_zero = sem("zeros_ready")
        s_fin = sem("final_ready")
        s_scattered = sem("scattered")
        s_bf = sem("bf16_tables_ready")

        class Steps:

            def __init__(self, name):
                self.w1 = [sem(f"{name}_w1_loaded{k}") for k in range(KC)]
                self.w2 = [sem(f"{name}_w2_loaded{k}") for k in range(FQ // 2)]
                self.b1 = sem(f"{name}_b1_loaded")
                self.b1_used = sem(f"{name}_b1_used")
                self.w1_used = sem(f"{name}_w1_used")
                self.w2_used = sem(f"{name}_w2_used")
                self.slots = sem(f"{name}_slots_ready")
                self.wslots = sem(f"{name}_gated_slots_ready")
                self.gathered = sem(f"{name}_gathered")
                self.x = sem(f"{name}_x_stored")
                self.g = sem(f"{name}_gate_clamped")
                self.sig = sem(f"{name}_sigmoid_done")
                self.act = sem(f"{name}_act_ready")
                self.at = sem(f"{name}_act_transposed")
                self.at_lo = sem(f"{name}_act_low_stored")
                self.at_hi = sem(f"{name}_act_high_stored")
                self.ye = sem(f"{name}_y_stored")
                self.sw = sem(f"{name}_scatter_transposed")
                self.swe = sem(f"{name}_scatter_stored")
                self.chain = sem(f"{name}_vector_steps")

        main, extra = Steps("main"), Steps("extra")

        def load_w1(sp, s, e, k):
            sp.dma_start(w1_ring[:, k, :], w1[bass.ds(e, 1), k * P:(k + 1) * P, :].rearrange("e p n -> p (e n)"))\
                .then_inc(s.w1[k], 16)

        def load_w2(sp, s, e, j):
            src = w2[bass.ds(e, 1), 2 * j * P:(2 * j + 2) * P, :].rearrange("e (q p) n -> p (e q) n", p=P)
            sp.dma_start(w2_ring[:, 2 * j:2 * j + 2, :], src).then_inc(s.w2[j], 16)

        def load_b1(sp, s, e):
            sp.dma_start(b1_row[0:1, :], b1[bass.ds(e, 1), :]).then_inc(s.b1, 16)

        block = ctx.enter_context(nc.Block())

        @block.sync
        def _(sp):
            for t in range(TT):
                sp.dma_start(xb[:, t, :], x_in[t * P:(t + 1) * P, :]).then_inc(s_x[t], 16)

            def load_win(g):
                if g >= W_BUFS:
                    sp.wait_ge(s_proj, g - W_BUFS + 1)
                for half in range(2):
                    src = w_in[half * HALF:(half + 1) * HALF, GROUP_COLS[g]:GROUP_COLS[g] + HALF]
                    sp.dma_start(win[g % W_BUFS][:, 4 * half:4 * half + 4, :],
                                 src.rearrange("(k p) n -> p k n", p=P)).then_inc(s_win[g % W_BUFS], 16)

            for g in range(18):
                load_win(g)
                if g == W_BUFS:
                    for t in range(TT):
                        sp.dma_start(xb[:, t, :], x_in[t * P:(t + 1) * P, :]).then_inc(s_x[t], 16)
            sp.wait_ge(s_rs, RH)
            sp.dma_start(watt, w_att.rearrange("(k p) n -> p k n", p=P)).then_inc(s_watt, 16)
            sp.wait_ge(s_ro, TT)
            for half in range(2):
                sp.dma_start(wret[:, 4 * half:4 * half + 4, :],
                             w_ret[half * HALF:(half + 1) * HALF, :].rearrange("(k p) n -> p k n", p=P))\
                    .then_inc(s_wret, 16)
            load_win(18)
            sp.dma_start(wout[:, 0:5, :], w_out[0:5 * P, :].rearrange("(k p) n -> p k n", p=P)).then_inc(s_wouta, 16)
            for k in range(KC):
                if k < 2:
                    sp.wait_ge(s_proj, 17)
                elif k < 4:
                    sp.wait_ge(s_proj, 18)
                elif k < 6:
                    sp.wait_ge(s_proj, 19)
                load_w1(sp, main, 0, k)
            sp.dma_start(wout[:, 5:8, :], w_out[5 * P:D, :].rearrange("(k p) n -> p k n", p=P)).then_inc(s_woutb, 16)
            sp.wait_ge(s_br, 4)
            for j in range(FQ // 2):
                load_w2(sp, main, 0, j)
            sp.wait_ge(s_zero, 1)
            load_b1(sp, main, 0)
            with sp.Fori(1, N_EXP) as e:
                sp.wait_ge(main.b1_used, e)
                load_b1(sp, main, e)
                for k in range(KC):
                    sp.wait_ge(main.w1_used, e * KC - (KC - 1 - k))
                    load_w1(sp, main, e, k)
                for j in range(FQ // 2):
                    sp.wait_ge(main.w2_used, e * (FQ // 2) - (FQ // 2 - 1 - j))
                    load_w2(sp, main, e, j)
            sp.wait_ge(main.w1_used, N_EXP * KC)
            sp.wait_ge(main.w2_used, N_EXP * (FQ // 2))
            sp.wait_ge(s_table, 1)
            n = sp.value_load(list_i[0:1, 0:1], min_val=0, max_val=MAX_EXTRA)
            with sp.If(n > 0):
                with sp.Fori(0, n) as i:
                    sp.wait_ge(s_scattered, i + N_EXP + 1)
                    e = sp.value_load(list_i[0:1, bass.ds(i + 32, 1)], min_val=0, max_val=N_EXP - 1)
                    load_b1(sp, extra, e)
                    for k in range(KC):
                        load_w1(sp, extra, e, k)
                    for j in range(FQ // 2):
                        load_w2(sp, extra, e, j)
            sp.wait_ge(s_fin, TT)
            sp.dma_start(out.rearrange("(t p) d -> p t d", p=P), xb[:, :, :]).then_inc(s_out, 16)
            sp.wait_ge(s_out, 16)

        @block.gpsimd
        def _(pool):
            pool.wait_ge(s_tabd, 1)
            pool.dma_start(scratch, tab_sb).then_inc(s_tab, 16)
            pool.wait_ge(s_tab, 16)
            pool.dma_start(toep_up.rearrange("p (h c) -> p h c", h=N_ATT_HEADS),
                           bass.AP(scratch.tensor, 0, [[1, P], [384, N_ATT_HEADS], [1, T]])).then_inc(s_toep, 16)
            pool.wait_ge(s_last, 16)
            pool.tensor_copy(before_bf[:, :], lasting[:, P:2 * P]).then_inc(s_bf, 1)
            pool.tensor_copy(ones_bf[:, :], lasting[:, 2 * P:3 * P]).then_inc(s_bf, 1)
            pool.wait_ge(s_wo, TT)
            pool.memset(b1_row, 0.0).then_inc(s_zero, 1)
            pool.memset(sc_w, 0.0).then_inc(main.swe, 1)
            pool.memset(y_sb, 0.0).then_inc(main.ye, 1)

        @block.scalar
        def _(act):
            act.dma_start(lasting[:, :], c_lasting).then_inc(s_last, 16)
            act.dma_start(gain[:, :], bass.AP(g_mix.tensor, 0, [[0, P], [1, D]])).then_inc(s_gain, 16)
            act.dma_start(rel_sb, rel_bias).then_inc(s_biasin, 16)
            act.dma_start(onehot_sb, c_onehot).then_inc(s_biasin, 16)
            act.dma_start(mask_sb, c_mask).then_inc(s_biasin, 16)
            act.dma_start(early, c_early).then_inc(s_early, 16)
            for t in range(TT):
                act.wait_ge(s_x[t], 16)
                if t:
                    act.wait_ge(s_sq, t)
                act.activation(gr[:, 0, :], xb[:, t, :], ACT.Square, accum_out=ssq[:, t:t + 1]).then_inc(s_sq, 1)
            act.wait_ge(s_ms, 1)
            act.activation(rstd, rstd, ACT.Sqrt).then_inc(s_root, 1)
            act.dma_start(decay, c_decay.rearrange("p (h i) -> p h i", h=RH)).then_inc(s_decay, 16)
            act.dma_start(wr_sb[:, :, :], w_router.rearrange("(k p) e -> p k e", p=P)).then_inc(s_small, 16)
            act.dma_start(br_sb[:, :], bass.AP(b_router.tensor, 0, [[0, P], [1, N_EXP]])).then_inc(s_small, 16)
            act.dma_start(item_sb[:, :], c_item).then_inc(s_small, 16)
            act.dma_start(expert_sb[:, :], c_expert).then_inc(s_small, 16)
            act.wait_ge(s_h, TT)
            act.dma_start(gain[:, :], bass.AP(g_ffn.tensor, 0, [[0, P], [1, D]])).then_inc(s_gain, 16)
            for n in range(6):
                act.wait_ge(s_flip, n + 1)
                act.activation(toep[:, 2 * n:2 * n + 2, :].rearrange("p h c -> p (h c)"), bank(4 + n % 4), ACT.Copy)\
                    .then_inc(s_flipe, 1)

            def store_projection(g):
                b = 2 * (g % 2)
                act.wait_ge(s_proj, g + 1)
                if g < 8:
                    act.activation(A_QK[:, g * 1024:(g + 1) * 1024], bank(b, 2), ACT.Copy).then_inc(s_proje, 1)
                elif g < 11:
                    act.activation(vA[:, :, (g - 8) * HALF:(g - 7) * HALF], ps[:, b:b + 2, :], ACT.Copy).then_inc(s_proje, 1)
                elif g < 13:
                    act.activation(vR[:, :, (g - 11) * HALF:(g - 10) * HALF], ps[:, b:b + 2, :], ACT.Copy).then_inc(s_proje, 1)
                elif g < 15:
                    if g == 13:
                        act.wait_ge(s_pt, SLOTS * GROUPS)
                    act.activation(gr[:, :, (g - 13) * HALF:(g - 12) * HALF], ps[:, b:b + 2, :], ACT.Silu).then_inc(s_proje, 1)
                else:
                    to = (gateA, gateR)[(g - 15) // 2][:, 4 * ((g - 15) % 2):4 * ((g - 15) % 2) + 4, :]
                    act.activation(to.rearrange("p c t -> p (c t)"), bank(b, 2), ACT.Sigmoid).then_inc(s_proje, 1)

            def exps(s):
                act.wait_ge(s_max, s + 1)
                act.activation(probs[:, s % 2, :, 0:P], probs[:, s % 2, :, 0:P], ACT.Exp,
                               bias=negmax[:, 2 * s:2 * s + 1], accum_out=denom[:, 2 * s:2 * s + 1]).then_inc(s_exp, 1)
                act.activation(probs[:, s % 2, :, P:384], probs[:, s % 2, :, P:384], ACT.Exp,
                               bias=negmax[:, 2 * s + 1:2 * s + 2],
                               accum_out=denom[:, 2 * s + 1:2 * s + 2]).then_inc(s_exp, 1)

            def store_pt(s):
                for g in range(GROUPS):
                    act.wait_ge(s_pt, GROUPS * s + g + 1)
                    if s >= 2:
                        act.wait_ge(s_pv, s - 1)
                    act.activation(ptb[:, s % 2, g, :], ps[:, 4 + g, 0:384], ACT.Copy).then_inc(s_pte, 1)

            for g in range(10):
                store_projection(g)
            exps(0)
            for s in range(SLOTS):
                store_projection(10 + s)
                store_pt(s)
                if s + 1 < SLOTS:
                    exps(s + 1)
            store_projection(14)
            act.wait_ge(s_rv, 1)
            act.activation(rrstd, rrstd, ACT.Sqrt).then_inc(s_rr, 1)
            store_projection(15)
            store_projection(16)
            for b in range(4):
                act.wait_ge(s_rt, b + 1)
                act.activation(retT[:, 2 * b:2 * b + 2, :].rearrange("p c t -> p (c t)"), bank(4 + b), ACT.Copy)\
                    .then_inc(s_rte, 1)
            store_projection(17)
            store_projection(18)
            for t in range(TT):
                act.wait_ge(s_x2, t + 1)
                if t:
                    act.wait_ge(s_sq, TT + t)
                act.activation(junk, xb[:, t, :], ACT.Square, accum_out=ssq[:, t:t + 1]).then_inc(s_sq, 1)
            act.wait_ge(s_ms, 2)
            act.activation(rstd, rstd, ACT.Sqrt).then_inc(s_root, 1)
            for b in range(4):
                act.wait_ge(s_xt, b + 1)
                act.activation(xnT[:, 2 * b:2 * b + 2, :].rearrange("p c t -> p (c t)"), bank(b), ACT.Copy)\
                    .then_inc(s_xte, 1)
            act.dma_start(b2_sb, b2).then_inc(s_b2, 16)
            for t in range(TT):
                act.wait_ge(s_tk, t + 1)
                act.activation(top[:, t * 64 + 16:t * 64 + 20], top[:, t * 64:t * 64 + 4], ACT.Exp,
                               bias=top[:, t * 64 + 24:t * 64 + 25],
                               accum_out=top[:, t * 64 + 25:t * 64 + 26]).then_inc(s_tke, 1)
            act.wait_ge(s_h, 2 * TT)
            act.dma_start(gain[:, :], bass.AP(g_final.tensor, 0, [[0, P], [1, D]])).then_inc(s_gain, 16)
            act.wait_ge(s_gtp, 1)
            act.activation(gT, ps[0:N_EXP, 6, 0:T], ACT.Copy).then_inc(s_gte, 1)

            def store_x(s, i):
                act.wait_ge(s.gathered, i + 1)
                act.activation(XT.rearrange("p k s -> p (k s)"), bank(6), ACT.Copy).then_inc(s.x, 1)

            def sigmoid(s, i):
                act.wait_ge(s.g, i + 1)
                act.activation(sg, gl, ACT.Sigmoid, scale=ALPHA).then_inc(s.sig, 1)

            def store_act_low(s, i):
                act.wait_ge(s.at, i * 2 + 1)
                act.activation(actT[:, 0:256], ps[:, 6, 0:256], ACT.Copy).then_inc(s.at_lo, 1)

            store_x(main, 0)
            with act.Fori(0, N_EXP) as i:
                sigmoid(main, i)
                store_x(main, i + 1)
                store_act_low(main, i)
            act.wait_ge(s_table, 1)
            n = act.value_load(list_i[0:1, 0:1], min_val=0, max_val=MAX_EXTRA)
            with act.If(n > 0):
                with act.Fori(0, n) as i:
                    store_x(extra, i)
                    sigmoid(extra, i)
                    store_act_low(extra, i)
            for t in range(TT):
                act.wait_ge(s_x2, TT + t + 1)
                if t:
                    act.wait_ge(s_sq, 2 * TT + t)
                act.activation(junk, xb[:, t, :], ACT.Square, accum_out=ssq[:, t:t + 1]).then_inc(s_sq, 1)
            act.wait_ge(s_ms, 3)
            act.activation(rstd, rstd, ACT.Sqrt).then_inc(s_root, 1)

        @block.tensor
        def _(pe):
            def transposes(src, first_bank, done):
                for c in range(KC):
                    for t in range(TT):
                        o = (c % 2) * T + t * P
                        mm = pe.transpose(ps[:, first_bank + c // 2, o:o + P], src[:, t, c * P:(c + 1) * P], ident)
                    if c % 2:
                        mm.then_inc(done, 1)

            pe.wait_ge(s_last, 16)
            pe.wait_ge(s_biasin, 48)
            pe.matmul(ps[0:N_ATT_HEADS, 7, 0:384], rel_sb, onehot_sb, start=True, stop=True).then_inc(s_tabp, 1)
            pe.wait_ge(s_h, TT)
            transposes(xb, 0, s_ht)
            pe.wait_ge(s_early, 16)
            pe.wait_ge(s_toep, 16)
            for n in range(6):
                if n >= 4:
                    pe.wait_ge(s_flipe, n - 3)
                else:
                    pe.wait_ge(s_tabd, 1)
                pe.matmul(bank(4 + n % 4), flip, toep_up[:, n * HALF:(n + 1) * HALF], start=True, stop=True)\
                    .then_inc(s_flip, 1)

            def project(g):
                w, b = win[g % W_BUFS], 2 * (g % 2)
                pe.wait_ge(s_win[g % W_BUFS], 32 * (g // W_BUFS + 1))
                if g == 0:
                    pe.wait_ge(s_hte, 4)
                elif g >= 2:
                    pe.wait_ge(s_proje, g - 1)
                if g < 8 or g >= 15:
                    for c in range(4):
                        for k in range(KC):
                            mm = pe.matmul(ps[:, b + c // 2, (c % 2) * T:(c % 2 + 1) * T], w[:, k, c * P:(c + 1) * P],
                                           hT[:, k, :], start=(k == 0), stop=(k == KC - 1))
                else:
                    for t in range(TT):
                        for k in range(KC):
                            mm = pe.matmul(bank(b + t), hT[:, k, t * P:(t + 1) * P], w[:, k, :],
                                           start=(k == 0), stop=(k == KC - 1))
                mm.then_inc(s_proj, 1)

            def rotate_pairs():
                pe.wait_ge(s_early, 16)
                pe.wait_ge(s_proje, 8)
                pe.wait_ge(s_flipe, 6)
                for i in range(2):
                    for h in range(RH):
                        mm = pe.matmul(psf[:, 4 * HALF + (4 * i + h) * T:4 * HALF + (4 * i + h + 1) * T], rot,
                                       qk[:, 6 + i, h, :], start=True, stop=True)
                    mm.then_inc(s_rotm, 1)

            def scores(s):
                if s == 0:
                    pe.wait_ge(s_rotd, 3)
                else:
                    pe.wait_ge(s_pte, GROUPS * s)
                for g in range(GROUPS):
                    pe.matmul(psf[:, 4 * HALF + g * T:4 * HALF + (g + 1) * T], qk[:, g, s, P:T], qk[:, 3 + g, s, :],
                              start=True, stop=True)
                for g in range(GROUPS):
                    mm = pe.matmul(ps[:, 6, g * P:(g + 1) * P], qk[:, g, s, 0:P], qk[:, 3 + g, s, 0:P],
                                   start=True, stop=True)
                mm.then_inc(s_sc, 1)

            def transpose_probs(s):
                pe.wait_ge(s_diag, 2 * (s + 1))
                for g in range(GROUPS):
                    for n, (tile, k) in enumerate(((0, 0), (1, 0), (1, 1))):
                        mm = pe.matmul(ps[:, 4 + g, n * P:(n + 1) * P], probs[:, s % 2, g, (tile + k) * P:(tile + k + 1) * P],
                                       diag[:, 2 * s + tile, :], start=True, stop=True)
                    mm.then_inc(s_pt, 1)

            def attend(s):
                pe.wait_ge(s_pte, GROUPS * (s + 1))
                pe.wait_ge(s_proje, 11)
                if s == SLOTS - 1:
                    pe.wait_ge(s_rse, RH)
                elif s:
                    pe.wait_ge(s_pve, s)
                for g in range(GROUPS):
                    c = (g * SLOTS + s) * P
                    pe.matmul(ps[:, 7, 0:T], vA[:, 0, c:c + P], ptb[:, s % 2, g, 0:T],
                              start=(g == 0), stop=False)
                    mm = pe.matmul(ps[:, 7, P:T], vA[:, 1, c:c + P], ptb[:, s % 2, g, T:384],
                                   start=False, stop=(g == GROUPS - 1))
                mm.then_inc(s_pv, 1)

            def ret_scores():
                pe.wait_ge(s_rotd, 4)
                pe.wait_ge(s_pte, GROUPS * SLOTS)
                for h in range(RH):
                    if h == 3:
                        pe.wait_ge(s_pve, 3)
                    pe.matmul(ps[:, 4 + h, 0:T], qk[:, 7, h, 0:P], qk[:, 6, h, :], start=True, stop=True)
                    pe.matmul(ps[:, 4 + h, T:384], qk[:, 7, h, P:T], qk[:, 6, h, P:T], start=True, stop=True)\
                        .then_inc(s_rs, 1)

            def ret_out():
                pe.wait_ge(s_rse, RH)
                pe.wait_ge(s_proje, 13)
                for t in range(TT):
                    if t == 1:
                        pe.wait_ge(s_pve, 4)
                    for h in range(RH):
                        o = psf[:, (4 + 2 * t) * HALF + h * DV:(4 + 2 * t) * HALF + (h + 1) * DV]
                        mm = pe.matmul(o, st[:, h, t * P:(t + 1) * P], vR[:, 0, h * DV:(h + 1) * DV],
                                       start=True, stop=(t == 0))
                        if t == 1:
                            mm = pe.matmul(o, st[:, h, T:384], vR[:, 1, h * DV:(h + 1) * DV], start=False, stop=True)
                    mm.then_inc(s_ro, 1)

            for g in range(9):
                project(g)
            rotate_pairs()
            project(9)
            scores(0)
            for s in range(SLOTS):
                project(10 + s)
                transpose_probs(s)
                if s >= 1:
                    attend(s - 1)
                if s + 1 < SLOTS:
                    scores(s + 1)
            ret_scores()
            project(14)
            attend(SLOTS - 1)
            ret_out()
            project(15)
            project(16)
            pe.wait_ge(s_rg, 2)
            transposes(gr, 4, s_rt)
            project(17)
            project(18)
            pe.wait_ge(s_watt, 16)
            pe.wait_ge(s_pve, SLOTS)
            pe.wait_ge(s_wret, 32)
            pe.wait_ge(s_rte, 4)
            for j in range(4):
                b = 2 * ((j + 1) % 2)
                if j < 2:
                    pe.wait_ge(s_proje, 18 + j)
                else:
                    pe.wait_ge(s_mg, j - 1)
                for i in range(2):
                    c = 2 * j + i
                    for k in range(4):
                        pe.matmul(ps[:, b, i * T:(i + 1) * T], watt[:, k, c * P:(c + 1) * P], attT[:, k, :],
                                  start=(k == 0), stop=(k == 3))
                for i in range(2):
                    c = 2 * j + i
                    for k in range(KC):
                        mm = pe.matmul(ps[:, b + 1, i * T:(i + 1) * T], wret[:, k, c * P:(c + 1) * P], retT[:, k, :],
                                       start=(k == 0), stop=(k == KC - 1))
                mm.then_inc(s_br, 1)
            pe.wait_ge(s_wouta, 16)
            pe.wait_ge(s_woutb, 16)
            for k in range(KC):
                pe.wait_ge(s_mg, k // 2 + 1)
                for t in range(TT):
                    for half in range(2):
                        mm = pe.matmul(bank(4 + 2 * t + half), mergedT[:, k, t * P:(t + 1) * P],
                                       wout[:, k, half * HALF:(half + 1) * HALF], start=(k == 0), stop=(k == KC - 1))
                    if k == KC - 1:
                        mm.then_inc(s_wo, 1)
            pe.wait_ge(s_h, 2 * TT)
            transposes(xn, 0, s_xt)
            pe.wait_ge(s_small, 64)
            pe.wait_ge(s_xte, 4)
            pe.wait_ge(s_x2, TT)
            for t in range(TT):
                for k in range(KC):
                    mm = pe.matmul(ps[:, 4, t * N_EXP:(t + 1) * N_EXP], xnT[:, k, t * P:(t + 1) * P], wr_sb[:, k, :],
                                   start=(k == 0), stop=(k == KC - 1))
            mm.then_inc(s_lg, 1)
            pe.wait_ge(s_bf, 2)
            pe.wait_ge(s_mask, TT)
            pe.matmul(ps[:, 5, 0:32], before_bf[:, :], mask_bf[:, 0, :], start=True, stop=True)
            pe.matmul(ps[:, 5, 32:64], before_bf[:, :], mask_bf[:, 1, :], start=True, stop=False)
            pe.matmul(ps[:, 5, 32:64], ones_bf[:, :], mask_bf[:, 0, :], start=False, stop=True)
            pe.matmul(ps[:, 5, 64:96], ones_bf[:, :], mask_bf[:, 0, :], start=True, stop=False)
            pe.matmul(ps[:, 5, 64:96], ones_bf[:, :], mask_bf[:, 1, :], start=False, stop=True).then_inc(s_pos, 1)
            for t in range(TT):
                mm = pe.transpose(ps[0:N_EXP, 6, t * P:(t + 1) * P], gates[:, t, 0:N_EXP], ident)
            mm.then_inc(s_gtp, 1)
            pe.wait_ge(s_gte, 1)
            pe.wait_ge(s_b2, 16)
            for t in range(TT):
                for half in range(2):
                    mm = pe.matmul(bank(2 * t + half), gT[:, t * P:(t + 1) * P], b2_sb[:, half * HALF:(half + 1) * HALF],
                                   start=True, stop=True)
            mm.then_inc(s_bias2, 1)

            def gather(s, i):
                pe.wait_ge(s.slots, i + 1)
                for k in range(KC):
                    for part in range(3):
                        for t in range(TT):
                            mm = pe.matmul(ps[:, 6, k * CAP:(k + 1) * CAP], xs[:, part, t, k * P:(k + 1) * P],
                                           s_one[:, t, :], start=(part == 0 and t == 0), stop=(part == 2 and t == 1))
                mm.then_inc(s.gathered, 1)

            def hidden(s, i):
                pe.wait_ge(s.b1, i * 16 + 16)
                pe.wait_ge(s.x, i + 1)
                for c in range(4):
                    o = ps[CAP * (c % 2):CAP * (c % 2) + CAP, 4 + c // 2, :]
                    mm = pe.matmul(o, first_row, b1_row[:, c * HALF:(c + 1) * HALF], start=True, stop=False)
                mm.then_inc(s.b1_used, 1)
                for k in range(KC):
                    pe.wait_ge(s.w1[k], i * 16 + 16)
                    for c in range(4):
                        o = ps[CAP * (c % 2):CAP * (c % 2) + CAP, 4 + c // 2, :]
                        mm = pe.matmul(o, XT[:, k, :], w1_ring[:, k, c * HALF:(c + 1) * HALF],
                                       start=False, stop=(k == KC - 1))
                    mm.then_inc(s.w1_used, 1)

            def transpose_act(s, i):
                pe.wait_ge(s.act, i + 1)
                for j in range(4):
                    mm = pe.transpose(ps[:, 6 + j // 2, (j % 2) * P:(j % 2 + 1) * P], act_sb[:, j * P:(j + 1) * P], ident)
                    if j % 2:
                        mm.then_inc(s.at, 1)

            def project_down(s, i):
                pe.wait_ge(s.at_lo, i + 1)
                pe.wait_ge(s.at_hi, i + 1)
                for n, q in enumerate((0, 1, 2, 3, 4, 5, 6, 7)):
                    if q % 2 == 0:
                        pe.wait_ge(s.w2[q // 2], i * 16 + 16)
                    for c in range(2):
                        lhs = actT[:, (q % 4) * P + (q // 4) * CAP:(q % 4) * P + (q // 4) * CAP + CAP]
                        mm = pe.matmul(ps[CAP * c:CAP * c + CAP, 7, :], lhs, w2_ring[:, q, c * HALF:(c + 1) * HALF],
                                       start=(n == 0), stop=(n == FQ - 1))
                    if q % 2:
                        mm.then_inc(s.w2_used, 1)

            def transpose_slots(s, i):
                pe.wait_ge(s.wslots, i + 1)
                pe.wait_ge(s.at_lo, i + 1)
                for t in range(TT):
                    mm = pe.transpose(ps[:, 6, t * P:(t + 1) * P], s_w[:, t, :], ident)
                mm.then_inc(s.sw, 1)

            def scatter(s, i):
                pe.wait_ge(s.ye, i + 1)
                pe.wait_ge(s.swe, i + 1)
                for t in range(TT):
                    for c in range(2):
                        mm = pe.matmul(bank(2 * t + c), sc_w[:, c, t * P:(t + 1) * P], y_sb, start=False, stop=True,
                                       skip_group_check=True)
                mm.then_inc(s_scattered, 1)

            gather(main, 0)
            with pe.Fori(0, N_EXP) as i:
                hidden(main, i)
                pe.wait_ge(main.swe, i + 1)
                gather(main, i + 1)
                scatter(main, i)
                pe.wait_ge(main.x, i + 2)
                transpose_act(main, i)
                project_down(main, i)
                transpose_slots(main, i)
            scatter(main, N_EXP)
            pe.wait_ge(s_table, 1)
            n = pe.value_load(list_i[0:1, 0:1], min_val=0, max_val=MAX_EXTRA)
            with pe.If(n > 0):
                with pe.Fori(0, n) as i:
                    gather(extra, i)
                    hidden(extra, i)
                    transpose_act(extra, i)
                    project_down(extra, i)
                    transpose_slots(extra, i)
                    scatter(extra, i)

        @block.vector
        def _(dve):
            chain = [0]

            def link(ins):
                chain[0] += 1
                ins.then_inc(s_dve, 1)
                dve.wait_ge(s_dve, chain[0])

            def root_mean_square(n):
                dve.wait_ge(s_sq, n * TT)
                dve.tensor_scalar(rstd, ssq, 1.0 / D, EPS, ALU.mult, ALU.add).then_inc(s_ms, 1)
                dve.wait_ge(s_root, n)
                link(dve.reciprocal(rstd, rstd))

            dve.wait_ge(s_tabp, 1)
            dve.tensor_tensor(tab_sb, ps[0:N_ATT_HEADS, 7, 0:384], mask_sb, ALU.add).then_inc(s_tabd, 1)
            root_mean_square(1)
            dve.wait_ge(s_gain, 16)
            for t in range(TT):
                dve.scalar_tensor_tensor(xb[:, t, :], xb[:, t, :], rstd[:, t:t + 1], gain[:, :],
                                         ALU.mult, ALU.mult).then_inc(s_h, 1)
            for b in range(4):
                dve.wait_ge(s_ht, b + 1)
                dve.tensor_copy(hT[:, 2 * b:2 * b + 2, :].rearrange("p c t -> p (c t)"), bank(b)).then_inc(s_hte, 1)

            cos4 = cosT.rearrange("p (a t) -> p a t", a=1).broadcast_to([P, 4, T])
            sin4 = sinT.rearrange("p (a t) -> p a t", a=1).broadcast_to([P, 4, T])
            rt4 = rtmp.rearrange("p (a t) -> p a t", a=4)
            for i in range(2):
                dve.wait_ge(s_rotm, i + 1)
                dve.tensor_tensor(rt4, bank(4 + 2 * i, 2).rearrange("p (a t) -> p a t", a=4), sin4, ALU.mult)\
                    .then_inc(s_rotd, 1)
                link(dve.tensor_tensor(qk[:, 6 + i, :, :], qk[:, 6 + i, :, :], cos4, ALU.mult))
                dve.wait_ge(s_rotd, 2 * i + 1)
                dve.tensor_tensor(qk[:, 6 + i, :, :], qk[:, 6 + i, :, :], rt4, ALU.add).then_inc(s_rotd, 1)
                dve.wait_ge(s_rotd, 2 * i + 2)

            dve.wait_ge(s_flipe, 6)

            def store_scores(s):
                dve.wait_ge(s_sc, s + 1)
                if s >= 2:
                    dve.wait_ge(s_pt, GROUPS * (s - 1))
                p3 = psf[:, 4 * HALF:4 * HALF + GROUPS * T].rearrange("p (g k) -> p g k", g=GROUPS)
                p2 = ps[:, 6, 0:GROUPS * P].rearrange("p (g k) -> p g k", g=GROUPS)
                heads = toep[:, s:N_ATT_HEADS:SLOTS, :]
                b = s % 2
                dve.scalar_tensor_tensor(probs[:, b, :, P:384], p3, ATT_SCALE, heads, ALU.mult, ALU.add)
                link(dve.scalar_tensor_tensor(probs[:, b, :, 0:P], p2, ATT_SCALE, heads[:, :, P:T], ALU.mult, ALU.add))
                dve.tensor_reduce(maxes[:, 2 * s:2 * s + 1], probs[:, b, :, 0:P], AX.XY, ALU.max)
                link(dve.tensor_reduce(maxes[:, 2 * s + 1:2 * s + 2], probs[:, b, :, P:384], AX.XY, ALU.max))
                dve.tensor_scalar(negmax[:, 2 * s:2 * s + 2], maxes[:, 2 * s:2 * s + 2], -1.0, None, ALU.mult)\
                    .then_inc(s_max, 1)

            def softmax_scales(s):
                dve.wait_ge(s_exp, 2 * s + 2)
                link(dve.reciprocal(rden[:, 2 * s:2 * s + 2], denom[:, 2 * s:2 * s + 2]))
                for t in range(TT):
                    dve.tensor_scalar(diag[:, 2 * s + t, :], ident, rden[:, 2 * s + t:2 * s + t + 1], None, ALU.mult)\
                        .then_inc(s_diag, 1)

            def store_att(s):
                dve.wait_ge(s_pv, s + 1)
                dve.tensor_copy(attT[:, s, :], ps[:, 7, 0:T]).then_inc(s_pve, 1)

            dve.wait_ge(s_last, 16)
            for s in range(SLOTS):
                if s >= 2:
                    store_att(s - 2)
                store_scores(s)
                softmax_scales(s)
            store_att(2)
            dve.wait_ge(s_decay, 16)
            for h in range(RH):
                dve.wait_ge(s_rs, h + 1)
                dve.tensor_tensor(st[:, h, 0:T], ps[:, 4 + h, 0:T], decay[:, h, :], ALU.mult)
                dve.tensor_tensor(st[:, h, T:384], ps[:, 4 + h, T:384], decay[:, h, 0:P], ALU.mult).then_inc(s_rse, 1)
            store_att(3)

            def ret_head(t, h):
                return psf[:, (4 + 2 * t) * HALF + h * DV:(4 + 2 * t) * HALF + (h + 1) * DV]

            for t in range(TT):
                dve.wait_ge(s_ro, t + 1)
                for h in range(RH):
                    last = dve.bn_stats(bns[:, 4 * t + h, :], ret_head(t, h))
            link(last)
            for n in range(8):
                last = dve.bn_aggr(mv[:, n, :], bns[:, n, :])
            link(last)
            dve.tensor_scalar(rrstd, mv[:, :, 1], EPS, None, ALU.add).then_inc(s_rv, 1)
            dve.wait_ge(s_rr, 1)
            link(dve.reciprocal(rrstd, rrstd))
            dve.wait_ge(s_proje, 15)
            for t in range(TT):
                for h in range(RH):
                    n = 4 * t + h
                    last = dve.tensor_scalar(gr[:, t, h * DV:(h + 1) * DV], gr[:, t, h * DV:(h + 1) * DV],
                                             rrstd[:, n:n + 1], None, ALU.mult)
                link(last)
                for h in range(RH):
                    n = 4 * t + h
                    last = dve.scalar_tensor_tensor(gr[:, t, h * DV:(h + 1) * DV], ret_head(t, h), mv[:, n, 0:1],
                                                    gr[:, t, h * DV:(h + 1) * DV], ALU.subtract, ALU.mult)
                last.then_inc(s_rg, 1)

            for j in range(4):
                dve.wait_ge(s_br, j + 1)
                dve.wait_ge(s_proje, 18 + j // 2)
                b = 2 * ((j + 1) % 2)
                mg = mergedT[:, 2 * j:2 * j + 2, :].rearrange("p c t -> p (c t)")
                ga = gateA[:, 2 * j:2 * j + 2, :].rearrange("p c t -> p (c t)")
                gg = gateR[:, 2 * j:2 * j + 2, :].rearrange("p c t -> p (c t)")
                dve.tensor_tensor(mg, bank(b), ga, ALU.mult)
                link(dve.tensor_tensor(gg, bank(b + 1), gg, ALU.mult))
                dve.tensor_tensor(mg, mg, gg, ALU.add).then_inc(s_mg, 1)
            for t in range(TT):
                dve.wait_ge(s_x[t], 32)
                dve.wait_ge(s_wo, t + 1)
                dve.tensor_tensor(xb[:, t, :], xb[:, t, :], bank(4 + 2 * t, 2), ALU.add).then_inc(s_x2, 1)
            root_mean_square(2)
            dve.wait_ge(s_gain, 32)
            for t in range(TT):
                dve.scalar_tensor_tensor(xn[:, t, :], xb[:, t, :], rstd[:, t:t + 1], gain[:, :],
                                         ALU.mult, ALU.mult).then_inc(s_h, 1)
            dve.wait_ge(s_h, 2 * TT)
            rest = A_W[:, 0:2048]
            xn_f = xn.rearrange("p t d -> p (t d)")
            part = [xs[:, n, :, :].rearrange("p t d -> p (t d)") for n in range(3)]
            rest = A_W[:, 2048:4096]
            link(dve.tensor_copy(part[0], xn_f))
            link(dve.tensor_tensor(rest, xn_f, part[0], ALU.subtract))
            link(dve.tensor_copy(part[1], rest))
            link(dve.tensor_tensor(rest, rest, part[1], ALU.subtract))
            link(dve.tensor_copy(part[2], rest))
            dve.wait_ge(s_small, 64)
            dve.wait_ge(s_lg, 1)
            lg = [top[:, t * 64 + 32:t * 64 + 64] for t in range(TT)]
            for t in range(TT):
                last = dve.tensor_tensor(lg[t], ps[:, 4, t * N_EXP:(t + 1) * N_EXP], br_sb[:, :], ALU.add)
            link(last)
            for t in range(TT):
                last = dve.max(top[:, t * 64:t * 64 + 8], lg[t])
            link(last)
            for t in range(TT):
                dve.tensor_scalar(top[:, t * 64 + 24:t * 64 + 25], top[:, t * 64:t * 64 + 1], -1.0, None, ALU.mult)\
                    .then_inc(s_tk, 1)
                last = dve.max_index(top[:, t * 64 + 8:t * 64 + 16].bitcast(U32), top[:, t * 64:t * 64 + 8], lg[t])
            link(last)
            chosen = A_W[:, 4096:4096 + 2 * TT * TOP_K * N_EXP].rearrange("p (m t j e) -> p m t j e", m=2, t=TT, j=TOP_K)
            for t in range(TT):
                last = dve.tensor_copy(top[:, t * 64 + 20:t * 64 + 24], top[:, t * 64 + 8:t * 64 + 12].bitcast(U32))
            link(last)
            dve.wait_ge(s_tke, TT)
            for t in range(TT):
                last = dve.reciprocal(top[:, t * 64 + 26:t * 64 + 27], top[:, t * 64 + 25:t * 64 + 26])
            link(last)
            for t in range(TT):
                last = dve.tensor_scalar(top[:, t * 64 + 16:t * 64 + 20], top[:, t * 64 + 16:t * 64 + 20],
                                         top[:, t * 64 + 26:t * 64 + 27], None, ALU.mult)
            link(last)
            for t in range(TT):
                for j in range(TOP_K):
                    idx = top[:, t * 64 + 20 + j:t * 64 + 21 + j]
                    dve.tensor_scalar(chosen[:, 0, t, j, :], expert_sb[:, :], idx, None, ALU.is_equal)
                    last = dve.tensor_scalar(chosen[:, 1, t, j, :], expert_sb[:, :], idx,
                                             top[:, t * 64 + 16 + j:t * 64 + 17 + j], ALU.is_equal, ALU.mult)
            link(last)
            for t in range(TT):
                dve.tensor_reduce(gates[:, t, 0:N_EXP], chosen[:, 1, t, :, :].rearrange("p j e -> p e j"), AX.X, ALU.add)
                last = dve.tensor_reduce(mask_f[:, t, :], chosen[:, 0, t, :, :].rearrange("p j e -> p e j"), AX.X, ALU.add)
            link(last)
            for t in range(TT):
                dve.tensor_copy(mask_bf[:, t, :], mask_f[:, t, :]).then_inc(s_mask, 1)
            for b in range(1, 4):
                dve.tensor_copy(gates[:, :, b * N_EXP:(b + 1) * N_EXP], gates[:, :, 0:N_EXP])
            dve.wait_ge(s_pos, 1)
            for t in range(TT):
                last = dve.scalar_tensor_tensor(posm[:, t, 0:N_EXP], ps[:, 5, t * 32:(t + 1) * 32], 1.0, mask_f[:, t, :],
                                                ALU.add, ALU.mult)
            link(last)
            for b in (3, 2, 1):
                dve.tensor_scalar(posm[:, :, b * N_EXP:(b + 1) * N_EXP], posm[:, :, 0:N_EXP], -1.0 - b * CAP, None, ALU.add)
            link(dve.tensor_scalar(lists[0:1, 96:128], ps[0:1, 5, 64:96], 0.0, None, ALU.add))
            link(dve.tensor_scalar(posm[:, :, 0:N_EXP], posm[:, :, 0:N_EXP], -1.0, None, ALU.add))
            keys = top[0:1, 0:128]
            for b in range(4):
                last = dve.tensor_scalar(keys[:, b * N_EXP:(b + 1) * N_EXP], lists[0:1, 96:128],
                                         float(b * CAP) if b else 1.0e9, None, ALU.is_gt)
            link(last)
            link(dve.tensor_reduce(lists[0:1, 64:65], keys, AX.X, ALU.add))
            link(dve.tensor_copy(list_i[0:1, 0:1], lists[0:1, 64:65]))
            link(dve.tensor_tensor(keys, keys, item_sb[:, :], ALU.mult))
            link(dve.max(lists[0:1, 64:72], keys))
            link(dve.match_replace(keys, lists[0:1, 64:72], keys, 0.0))
            link(dve.max(lists[0:1, 72:80], keys))
            link(dve.tensor_scalar(lists[0:1, 64:80], lists[0:1, 64:80], -1.0, float(P), ALU.mult, ALU.add))
            link(dve.tensor_scalar(lists[0:1, 64:80], lists[0:1, 64:80], float(P - 1), None, ALU.min))
            dve.tensor_copy(list_i[0:1, 16:32], lists[0:1, 64:80])
            for b in range(1, 4):
                last = dve.tensor_scalar(lists[0:1, 80:96] if b == 1 else lists[0:1, 96 + 16 * (b - 2):112 + 16 * (b - 2)],
                                         lists[0:1, 64:80], float(b * N_EXP), -float(N_EXP), ALU.is_ge, ALU.mult)
            link(last)
            for b in range(3):
                link(dve.tensor_tensor(lists[0:1, 64:80], lists[0:1, 64:80], lists[0:1, 80 + 16 * b:96 + 16 * b], ALU.add))
            dve.tensor_copy(list_i[0:1, 32:48], lists[0:1, 64:80]).then_inc(s_table, 1)
            dve.wait_ge(s_table, 1)

            def slots(s, i, col):
                for t in range(TT):
                    last = dve.tensor_scalar(s_one[:, t, :], slot_ids[:, 0:CAP], posm[:, t, bass.ds(col, 1)], None,
                                             ALU.is_equal)
                last.then_inc(s.slots, 1)

            def gated_slots(s, i, col):
                for t in range(TT):
                    last = dve.tensor_scalar(s_w[:, t, :], slot_ids, posm[:, t, bass.ds(col, 1)],
                                             gates[:, t, bass.ds(col, 1)], ALU.is_equal, ALU.mult)
                last.then_inc(s.wslots, 1)

            def activate(s, i):
                dve.wait_ge(s.w1_used, i * KC + KC)
                dve.tensor_scalar(gl, bank(4), LIMIT, None, ALU.min).then_inc(s.g, 1)
                dve.tensor_scalar(ul, bank(5), LIMIT, -LIMIT, ALU.min, ALU.max).then_inc(s.chain, 1)
                dve.wait_ge(s.chain, i * 2 + 1)
                dve.wait_ge(s.g, i + 1)
                dve.scalar_tensor_tensor(ul, ul, 1.0, gl, ALU.add, ALU.mult).then_inc(s.chain, 1)
                dve.wait_ge(s.chain, i * 2 + 2)
                dve.wait_ge(s.sig, i + 1)
                dve.tensor_tensor(act_sb, ul, sg, ALU.mult).then_inc(s.act, 1)

            def store_act_high(s, i):
                dve.wait_ge(s.at, i * 2 + 2)
                dve.tensor_copy(actT[:, 256:512], ps[:, 7, 0:256]).then_inc(s.at_hi, 1)

            def store_y(s, i):
                dve.wait_ge(s.w2_used, i * (FQ // 2) + FQ // 2)
                dve.tensor_copy(y_sb, bank(7)).then_inc(s.ye, 1)

            def store_scatter(s, i):
                dve.wait_ge(s.sw, i + 1)
                dve.tensor_copy(sc_w[0:CAP, 0, :], ps[0:CAP, 6, 0:T])
                dve.tensor_copy(sc_w[CAP:P, 1, :], ps[CAP:P, 6, 0:T]).then_inc(s.swe, 1)

            slots(main, 0, 0)
            with dve.Fori(0, N_EXP) as i:
                dve.wait_ge(main.gathered, i + 1)
                slots(main, i + 1, i + 1)
                gated_slots(main, i, i)
                activate(main, i)
                store_act_high(main, i)
                store_y(main, i)
                store_scatter(main, i)
            dve.wait_ge(s_scattered, N_EXP + 1)
            n = dve.value_load(list_i[0:1, 0:1], min_val=0, max_val=MAX_EXTRA)
            with dve.If(n > 0):
                with dve.Fori(0, n) as i:
                    item = dve.value_load(list_i[0:1, bass.ds(i + 16, 1)], min_val=0, max_val=P - 1)
                    slots(extra, i, item)
                    gated_slots(extra, i, item)
                    activate(extra, i)
                    store_act_high(extra, i)
                    store_y(extra, i)
                    store_scatter(extra, i)
                dve.wait_ge(s_scattered, n + N_EXP + 1)
                dve.memset(lists[0:1, 64:65], 0.0)
            for t in range(TT):
                dve.tensor_tensor(xb[:, t, :], xb[:, t, :], bank(2 * t, 2), ALU.add).then_inc(s_x2, 1)
            root_mean_square(3)
            dve.wait_ge(s_gain, 48)
            for t in range(TT):
                dve.scalar_tensor_tensor(xb[:, t, :], xb[:, t, :], rstd[:, t:t + 1], gain[:, :],
                                         ALU.mult, ALU.mult).then_inc(s_fin, 1)


_INS = ["x", "norm_mix_g", "w_in", "rel_bias", "w_att_branch", "w_ret_branch", "w_out", "norm_ffn_g",
        "w_router", "b_router", "w1", "b1", "w2", "b2", "norm_final_g"]


def kernel(**inputs):
    import numpy as _np
    import concourse.bacc as _bacc
    from concourse import mybir as _mybir
    from concourse.bass_utils import run_bass_kernel_spmd as _run

    nc = _bacc.Bacc("TRN2", target_bir_lowering=False, num_devices=1)
    arrays, args = {}, []

    def declare(name, a):
        arrays[name] = a
        args.append(nc.dram_tensor(name, a.shape, _mybir.dt.from_np(a.dtype), kind="ExternalInput").ap())

    for name in _INS:
        a = _np.asarray(inputs[name])
        if name not in ("rel_bias", "norm_final_g"):
            a = a[0]
        declare(f"in_{name}", _np.ascontiguousarray(a))
    for name, a in host_constants().items():
        declare(name, _np.ascontiguousarray(a))
    args.append(nc.dram_tensor("out_0", (T, D), F32, kind="ExternalOutput").ap())
    hybrid_block_kernel(nc, *args)
    r = _run(nc, [arrays], core_ids=[0])
    return _np.asarray(r.results[0]["out_0"]).reshape(1, T, D)
```

```python
from contextlib import ExitStack

import numpy as np

import concourse.bass as bass
from concourse import mybir

ALU = mybir.AluOpType
ACT = mybir.ActivationFunctionType
AX = mybir.AxisListType
F32 = mybir.dt.float32
F32R = mybir.dt.float32r
BF16 = mybir.dt.bfloat16
I32 = mybir.dt.int32
U32 = mybir.dt.uint32

P = 128
D = 1024
T = 256
KC = D // P
TT = T // P
EPS = 1e-5
HALF = 512

SLOTS = 4
GROUPS = 3
N_ATT_HEADS = SLOTS * GROUPS
WINDOWS = ((128, 1), (512, 4), (2048, 16))
ATT_SCALE = 128.0 ** -0.5
REL_BUCKETS, REL_MAX_DIST = 32, 2048
MASKED = -1.0e30
RH = 4
DV = 256

N_EXP = 32
TOP_K = 4
F = 1024
CAP = 64
FQ = F // P
LIMIT = 7.0
ALPHA = 1.702
MAX_EXTRA = 16

GROUP_COLS = [0, 512, 1024, 1536, 2048, 2560, 4608, 5120,
              3072, 3584, 4096, 5632, 6144, 6656, 7168,
              7680, 8192, 8704, 9216]
N_GROUPS = len(GROUP_COLS)
QK_GROUPS = 8
W_BUFS = 2
UNITS = 4
LAST_UNIT = N_GROUPS * UNITS


def host_constants():
    f = np.float32
    p = np.arange(P)
    t = np.arange(T)
    ident = np.eye(P, dtype=f)
    rot = np.zeros((P, P), f)
    rot[p[1::2], p[0::2]] = -1.0
    rot[p[0::2], p[1::2]] = 1.0
    inv = (f(10000.0) ** (-np.arange(0, P, 2, dtype=f) / f(P))).astype(f)
    ang = (t.astype(f)[:, None] * inv[None]).astype(f)
    cos = np.repeat(np.cos(ang).T, 2, axis=0).astype(f)
    sin = np.repeat(np.sin(ang).T, 2, axis=0).astype(f)
    log_g = np.log(1.0 - 2.0 ** (-5.0 - np.arange(RH)))
    dist = t[None, :] - p[:, None]
    decay = np.where(dist[:, None] >= 0, np.exp(np.maximum(dist, 0)[:, None] * log_g[None, :, None]), 0.0)
    decay = (decay * P ** -0.5).astype(f).reshape(P, RH * T)
    before = (p[:, None] < p[None, :]).astype(f)
    ones = np.ones((P, P), f)
    slot = np.tile(np.arange(CAP, dtype=f), (P, 2))
    first_row = np.zeros((P, CAP), f)
    first_row[0] = 1.0
    early = np.concatenate([rot, cos, sin, ident[::-1]], axis=1)
    lasting = np.concatenate([ident, before, ones, slot, first_row], axis=1)
    d = 255 - np.arange(384)
    exact = REL_BUCKETS // 2
    large = exact + (np.log(np.maximum(d, 1).astype(f) / f(exact)) / f(np.log(REL_MAX_DIST / exact))
                     * f(REL_BUCKETS - exact)).astype(np.int32)
    bucket = np.where(d < exact, np.maximum(d, 0), np.minimum(large, REL_BUCKETS - 1))
    onehot = (np.arange(REL_BUCKETS)[:, None] == bucket[None]).astype(f)
    mask = np.zeros((N_ATT_HEADS, 384), f)
    for g, (window, dilation) in enumerate(WINDOWS):
        seen = (d >= 0) & (d % dilation == 0) & (d <= window)
        mask[g * SLOTS:(g + 1) * SLOTS] = np.where(seen, 0.0, MASKED)
    item = np.tile((P - np.arange(P, dtype=f)), (1, 1))
    e_of = np.tile(np.arange(N_EXP, dtype=f), (P, 1))
    return {"c_early": early, "c_lasting": lasting, "c_decay": decay, "c_onehot": onehot,
            "c_mask": mask, "c_item": item, "c_expert": e_of}


def hybrid_block_kernel(nc, x_in, g_mix, w_in, rel_bias, w_att, w_ret, w_out, g_ffn, w_router, b_router,
                        w1, b1, w2, b2, g_final, c_early, c_lasting, c_decay, c_onehot, c_mask, c_item,
                        c_expert, out):
    with ExitStack() as ctx:
        def sb(name, shape, dt=F32):
            return ctx.enter_context(nc.sbuf_tensor(name, shape, dt))

        def sem(name):
            return ctx.enter_context(nc.semaphore(name))

        ps = ctx.enter_context(nc.psum_tensor("ps", [P, 8, HALF], F32))
        psf = ps[:, :, :].rearrange("p b n -> p (b n)")

        def bank(b, n=1):
            return psf[:, b * HALF:(b + n) * HALF]

        w1_ring = sb("w1_ring", [P, KC, 2 * F])
        w1_ring_end = nc.sbuf_base
        w2_ring = sb("w2_ring", [P, FQ, D])
        w1_flat = w1_ring[:, :, :].rearrange("p k n -> p (k n)")
        w2_flat = w2_ring[:, :, :].rearrange("p k n -> p (k n)")
        win = [w1_flat[:, b * KC * HALF:(b + 1) * KC * HALF].rearrange("p (k n) -> p k n", k=KC)
               for b in range(W_BUFS)]

        w_parts = nc.alloc_sbuf_tensor_at("w_parts", [P, UNITS, 2, 2, HALF], F32R, offset=w1_ring_end - 4 * UNITS * 4 * HALF)

        xb = sb("xb", [P, TT, D])
        hT_lo = nc.alloc_sbuf_tensor_at("hT_lo", [P, KC, T], F32R, offset=nc.sbuf_base - 4 * TT * D)
        A_QK = sb("A_QK", [P, 8192 + 2048])
        mergedT_lo = nc.alloc_sbuf_tensor_at("mergedT_lo", [P, KC, T], F32R, offset=nc.sbuf_base - 4 * 10240)
        A_W = sb("A_W", [P, 8192])
        hT_hi = nc.alloc_sbuf_tensor_at("hT_hi", [P, KC, T], F32R, offset=nc.sbuf_base - 4 * 8192 + 4 * 5120)
        A_PT = sb("A_PT", [P, 2304])
        mergedT_hi = nc.alloc_sbuf_tensor_at("mergedT_hi", [P, KC, T], F32R, offset=nc.sbuf_base - 4 * 2304)
        gr = sb("gr", [P, TT, D])
        attT = sb("attT", [P, SLOTS, T])
        gain = sb("gain", [P, D])
        lasting = sb("lasting", [P, 4 * P + CAP])
        before_bf = sb("before_bf", [P, P], BF16)
        ones_bf = sb("ones_bf", [P, P], BF16)
        wr_sb = sb("wr_sb", [P, KC, N_EXP])
        br_sb = sb("br_sb", [P, N_EXP])
        item_sb = sb("item_sb", [1, P])
        expert_sb = sb("expert_sb", [P, N_EXP])
        g_col = sb("g_col", [P, KC])
        zeros_bf = sb("zeros_bf", [P, HALF], BF16)
        small = sb("small", [P, 192])
        ident = lasting[:, 0:P]
        slot_ids = lasting[:, 3 * P:4 * P]
        first_row = lasting[:, 4 * P:4 * P + CAP]

        qk = A_QK[:, 0:8192].rearrange("p (g c t) -> p g c t", g=QK_GROUPS, c=4)
        early = A_QK[:, 8192:8192 + 768]
        rot, cosT, sinT, flip = early[:, 0:P], early[:, P:P + T], early[:, P + T:P + 2 * T], early[:, P + 2 * T:2 * P + 2 * T]
        gateA = A_QK[:, 0:2048].rearrange("p (c t) -> p c t", c=KC)
        gateR = A_QK[:, 2048:4096].rearrange("p (c t) -> p c t", c=KC)
        retT = A_QK[:, 4096:6144].rearrange("p (c t) -> p c t", c=KC)
        watt = A_QK[:, 6144:10240].rearrange("p (c n) -> p c n", c=4)
        vA = A_W[:, 0:3072].rearrange("p (t n) -> p t n", t=TT)
        vR = A_W[:, 3072:5120].rearrange("p (t n) -> p t n", t=TT)
        wout = A_W[:, 0:8192].rearrange("p (k n) -> p k n", k=KC)
        rel_sb = A_W[0:REL_BUCKETS, 7168:7168 + N_ATT_HEADS]
        onehot_sb = A_W[0:REL_BUCKETS, 7200:7584]
        mask_sb = A_W[0:N_ATT_HEADS, 7584:7968]
        tab_sb = w2_flat[0:N_ATT_HEADS, 7168:7552]
        toep_up = w2_flat[:, 4096:7168]
        ptb = A_PT[:, 0:2304].rearrange("p (b g q) -> p b g q", b=2, g=GROUPS)
        mergedT = gr[:, :, :].rearrange("p a n -> p (a n)").rearrange("p (c t) -> p c t", c=KC)
        toep = w2_flat[:, 0:3072].rearrange("p (h c) -> p h c", h=N_ATT_HEADS)
        decay = w2_flat[:, 3072:4096].rearrange("p (h i) -> p h i", h=RH)
        probs = w2_flat[:, 4096:6400].rearrange("p (b g k) -> p b g k", b=2, g=GROUPS)
        st = w2_flat[:, 6400:7936].rearrange("p (h i) -> p h i", h=RH)
        rtmp = w2_flat[:, 4096:5120]
        diag = gr[:, 1, :].rearrange("p (b q) -> p b q", b=8)
        wret = w2_flat.rearrange("p (k n) -> p k n", k=KC)

        xn = A_QK[:, 0:2048].rearrange("p (t d) -> p t d", t=TT)
        xT = A_QK[:, 2048:4096].rearrange("p (k t) -> p k t", k=KC)
        xs = A_QK[:, 4096:7168].bitcast(BF16).rearrange("p (s t d) -> p s t d", s=3, t=TT)
        junk = A_QK[:, 7168:8192]
        rest = A_W[:, 2048:4096].rearrange("p (t d) -> p t d", t=TT)
        posm = A_QK[:, 8192:8448].rearrange("p (t c) -> p t c", t=TT)
        gates = A_QK[:, 8448:8704].rearrange("p (t c) -> p t c", t=TT)
        top = A_QK[:, 8704:8960]
        b1_row = A_W[:, 0:2048]
        XT = A_W[:, 2048:2560].rearrange("p (k s) -> p k s", k=KC)
        gl = A_W[:, 2560:3072]
        ul = A_W[:, 3072:3584]
        sg = A_W[:, 3584:4096]
        act_sb = A_W[:, 4096:4608]
        actT = A_W[:, 4608:5120]
        y_sb = A_W[:, 5120:5632]
        sc_w = A_W[:, 5632:6144].rearrange("p (c t) -> p c t", c=2)
        s_w = A_W[:, 6144:6400].rearrange("p (t s) -> p t s", t=TT)
        s_one = A_W[:, 6400:6464].bitcast(BF16).rearrange("p (t s) -> p t s", t=TT)
        b2_row = A_W[:, 6464:7488]
        lists = A_W[0:1, 7744:7872]
        list_i = lists.bitcast(I32)
        mask_f = A_W[:, 4608:4672].rearrange("p (t e) -> p t e", t=TT)
        mask_bf = sb("mask_bf", [P, TT, N_EXP], BF16)

        scratch = nc.dram_tensor("bias_scratch", (N_ATT_HEADS, 384), F32, kind="Internal").ap()

        ssq, rstd = small[:, 0:2], small[:, 2:4]
        negmax = small[:, 8:16]
        denom = small[:, 16:24]
        rden = small[:, 24:32]
        bns = small[:, 32:80].rearrange("p (g s) -> p g s", g=8)
        mv = small[:, 80:96].rearrange("p (g s) -> p g s", g=8)
        rrstd = small[:, 96:104]
        maxes = small[:, 104:112]

        s_x = [sem(f"x_loaded{t}") for t in range(TT)]
        s_gain = sem("gain_loaded")
        s_early = sem("early_tables_loaded")
        s_last = sem("lasting_tables_loaded")
        s_biasin = sem("bias_tables_loaded")
        s_small = sem("router_loaded")
        s_decay = sem("decay_loaded")
        s_tab = sem("bias_table_stored")
        s_toep = sem("bias_tiles_loaded")
        s_flip = sem("bias_tiles_turned")
        s_flipe = sem("bias_tiles_stored")
        s_win = [[sem(f"w_in_loaded{b}_{half}") for half in range(2)] for b in range(W_BUFS)]
        s_wh = sem("w_in_high_parts")
        s_wl = sem("w_in_low_parts")
        s_wu = sem("w_in_units_used")
        s_watt = sem("w_att_loaded")
        s_wret = sem("w_ret_loaded")
        s_wouta = sem("w_out_head_loaded")
        s_woutb = sem("w_out_tail_loaded")
        s_out = sem("out_stored")

        s_dve = sem("vector_steps")
        s_sq = sem("squares_summed")
        s_root = sem("roots_done")
        s_ms = sem("mean_squares")
        s_h = sem("normed")
        s_ht = sem("normed_transposed")
        s_hte = sem("normed_transposed_high")
        s_htl = sem("normed_transposed_low")
        s_tabp = sem("bias_table_multiplied")
        s_tabd = sem("bias_table_ready")
        s_proje = sem("projection_stored")
        s_rotm = sem("rotated_pairs")
        s_rotd = sem("rotary_done")
        s_sc = sem("scores_done")
        s_sce = sem("scores_stored")
        s_max = sem("maxima_ready")
        s_exp = sem("exps_done")
        s_diag = sem("diag_ready")
        s_pt = sem("probs_transposed")
        s_pte = sem("probs_transposed_stored")
        s_pv = sem("att_done")
        s_pve = sem("att_stored")
        s_rs = sem("ret_scores_done")
        s_rse = sem("ret_scores_stored")
        s_ro = sem("ret_out_done")
        s_rv = sem("ret_variances_ready")
        s_rr = sem("ret_roots_done")
        s_rg = sem("ret_gated")
        s_rt = sem("ret_transposed")
        s_rte = sem("ret_transposed_stored")
        s_br = sem("branches_done")
        s_mg = sem("merged_ready")
        s_mh = sem("merged_high_parts")
        s_ml = sem("merged_low_parts")
        s_wo = sem("w_out_done")
        s_x2 = sem("residual_ready")
        s_xt = sem("x_transposed")
        s_xte = sem("x_transposed_stored")
        s_lg = sem("logits_done")
        s_tk = sem("top_values_ready")
        s_tke = sem("gate_exps_done")
        s_mask = sem("routing_masks_ready")
        s_pos = sem("positions_done")
        s_table = sem("routing_tables_ready")
        s_zero = sem("zeros_ready")
        s_fin = sem("final_ready")
        s_scattered = sem("scattered")
        s_wr = sem("router_scaled")
        s_split = sem("xn_parts_rounded")
        s_rest = sem("xn_rests_ready")
        s_bf = sem("bf16_tables_ready")

        class Steps:

            def __init__(self, name):
                self.w1 = [sem(f"{name}_w1_loaded{k}") for k in range(KC)]
                self.w2 = [sem(f"{name}_w2_loaded{k}") for k in range(FQ // 2)]
                self.b1 = sem(f"{name}_b1_loaded")
                self.b2 = sem(f"{name}_b2_loaded")
                self.b1_used = sem(f"{name}_b1_used")
                self.w1_used = sem(f"{name}_w1_used")
                self.w2_used = sem(f"{name}_w2_used")
                self.slots = sem(f"{name}_slots_ready")
                self.wslots = sem(f"{name}_gated_slots_ready")
                self.gathered = sem(f"{name}_gathered")
                self.x = sem(f"{name}_x_stored")
                self.g = sem(f"{name}_gate_clamped")
                self.sig = sem(f"{name}_sigmoid_done")
                self.act = sem(f"{name}_act_ready")
                self.at = sem(f"{name}_act_transposed")
                self.at_lo = sem(f"{name}_act_low_stored")
                self.at_hi = sem(f"{name}_act_high_stored")
                self.ye = sem(f"{name}_y_stored")
                self.sw = sem(f"{name}_scatter_transposed")
                self.swe = sem(f"{name}_scatter_stored")
                self.chain = sem(f"{name}_vector_steps")

        main, extra = Steps("main"), Steps("extra")

        def load_w1(sp, s, e, k):
            sp.dma_start(w1_ring[:, k, :], w1[bass.ds(e, 1), k * P:(k + 1) * P, :].rearrange("e p n -> p (e n)"))\
                .then_inc(s.w1[k], 16)

        def load_w2(sp, s, e, j):
            src = w2[bass.ds(e, 1), 2 * j * P:(2 * j + 2) * P, :].rearrange("e (q p) n -> p (e q) n", p=P)
            sp.dma_start(w2_ring[:, 2 * j:2 * j + 2, :], src).then_inc(s.w2[j], 16)

        def load_b1(sp, s, e):
            sp.dma_start(b1_row[0:1, :], b1[bass.ds(e, 1), :]).then_inc(s.b1, 16)

        def load_b2(sp, s, e):
            sp.dma_start(b2_row[0:1, :], b2[bass.ds(e, 1), :]).then_inc(s.b2, 16)

        def unit_views(u):
            raw = win[u // UNITS % W_BUFS][:, 2 * (u % UNITS):2 * (u % UNITS) + 2, :]
            return raw, w_parts[:, u % UNITS, 0], w_parts[:, u % UNITS, 1]

        def wout_views(k):
            parts = w_parts[:, k % UNITS, :, :, :].rearrange("p m a n -> p m (a n)")
            return wout[:, k, :], parts[:, 0], parts[:, 1]

        block = ctx.enter_context(nc.Block())

        @block.sync
        def _(sp):
            for t in range(TT):
                sp.dma_start(xb[:, t, :], x_in[t * P:(t + 1) * P, :]).then_inc(s_x[t], 16)
            sp.dma_start(gain[:, :], bass.AP(g_mix.tensor, 0, [[0, P], [1, D]])).then_inc(s_gain, 16)
            sp.dma_start(lasting[:, :], c_lasting).then_inc(s_last, 16)

            def load_win(g):
                if g >= W_BUFS:
                    sp.wait_ge(s_wl, UNITS * (g - W_BUFS + 1))
                for half in range(2):
                    src = w_in[half * HALF:(half + 1) * HALF, GROUP_COLS[g]:GROUP_COLS[g] + HALF]
                    sp.dma_start(win[g % W_BUFS][:, 4 * half:4 * half + 4, :],
                                 src.rearrange("(k p) n -> p k n", p=P)).then_inc(s_win[g % W_BUFS][half], 16)

            for g in range(17):
                load_win(g)
                if g == 0:
                    sp.dma_start(rel_sb, rel_bias).then_inc(s_biasin, 16)
                    sp.dma_start(onehot_sb, c_onehot).then_inc(s_biasin, 16)
                    sp.dma_start(mask_sb, c_mask).then_inc(s_biasin, 16)
                    sp.dma_start(early, c_early).then_inc(s_early, 16)
            sp.wait_ge(s_rs, RH)
            sp.dma_start(watt, w_att.rearrange("(k p) n -> p k n", p=P)).then_inc(s_watt, 16)
            load_win(17)
            sp.wait_ge(s_ro, TT)
            for half in range(2):
                sp.dma_start(wret[:, 4 * half:4 * half + 4, :],
                             w_ret[half * HALF:(half + 1) * HALF, :].rearrange("(k p) n -> p k n", p=P))\
                    .then_inc(s_wret, 16)
            load_win(18)
            sp.dma_start(wout[:, 0:5, :], w_out[0:5 * P, :].rearrange("(k p) n -> p k n", p=P)).then_inc(s_wouta, 16)
            sp.wait_ge(s_wl, UNITS * 18)
            for k in (2, 3):
                load_w1(sp, main, 0, k)
            sp.wait_ge(s_wl, LAST_UNIT)
            for k in (0, 1):
                load_w1(sp, main, 0, k)
            sp.wait_ge(s_wu, LAST_UNIT)
            for t in range(TT):
                sp.dma_start(xb[:, t, :], x_in[t * P:(t + 1) * P, :]).then_inc(s_x[t], 16)
            sp.dma_start(wout[:, 5:8, :], w_out[5 * P:D, :].rearrange("(k p) n -> p k n", p=P)).then_inc(s_woutb, 16)
            sp.wait_ge(s_br, 4)
            for j in range(FQ // 2):
                load_w2(sp, main, 0, j)
            sp.wait_ge(s_wo, TT)
            for k in range(4, KC):
                load_w1(sp, main, 0, k)
            sp.wait_ge(s_zero, 2)
            load_b1(sp, main, 0)
            load_b2(sp, main, 0)
            with sp.Fori(1, N_EXP) as e:
                sp.wait_ge(main.b1_used, e)
                load_b1(sp, main, e)
                for k in range(KC):
                    sp.wait_ge(main.w1_used, e * KC - (KC - 1 - k))
                    load_w1(sp, main, e, k)
                for j in range(FQ // 2):
                    sp.wait_ge(main.w2_used, e * (FQ // 2) - (FQ // 2 - 1 - j))
                    if j == 0:
                        load_b2(sp, main, e)
                    load_w2(sp, main, e, j)
            sp.wait_ge(main.w1_used, N_EXP * KC)
            sp.wait_ge(main.w2_used, N_EXP * (FQ // 2))
            sp.wait_ge(s_table, 1)
            n = sp.value_load(list_i[0:1, 0:1], min_val=0, max_val=MAX_EXTRA)
            with sp.If(n > 0):
                with sp.Fori(0, n) as i:
                    sp.wait_ge(s_scattered, i + N_EXP + 1)
                    e = sp.value_load(list_i[0:1, bass.ds(i + 32, 1)], min_val=0, max_val=N_EXP - 1)
                    load_b1(sp, extra, e)
                    load_b2(sp, extra, e)
                    for k in range(KC):
                        load_w1(sp, extra, e, k)
                    for j in range(FQ // 2):
                        load_w2(sp, extra, e, j)
            for t in range(TT):
                sp.wait_ge(s_fin, t + 1)
                sp.dma_start(out[t * P:(t + 1) * P, :], xb[:, t, :]).then_inc(s_out, 16)
            sp.wait_ge(s_out, 16 * TT)

        @block.gpsimd
        def _(pool):
            pool.wait_ge(s_tabd, 1)
            pool.dma_start(scratch, tab_sb).then_inc(s_tab, 16)
            pool.wait_ge(s_tab, 16)
            pool.dma_start(toep_up.rearrange("p (h c) -> p h c", h=N_ATT_HEADS),
                           bass.AP(scratch.tensor, 0, [[1, P], [384, N_ATT_HEADS], [1, T]])).then_inc(s_toep, 16)
            pool.wait_ge(s_last, 16)
            pool.tensor_copy(before_bf[:, :], lasting[:, P:2 * P]).then_inc(s_bf, 1)
            pool.tensor_copy(ones_bf[:, :], lasting[:, 2 * P:3 * P]).then_inc(s_bf, 1)
            pool.memset(zeros_bf[:, :], 0.0).then_inc(s_bf, 1)
            pool.wait_ge(s_wo, TT)
            pool.memset(b1_row, 0.0).then_inc(s_zero, 1)
            pool.memset(b2_row, 0.0).then_inc(s_zero, 1)
            pool.memset(sc_w, 0.0).then_inc(main.swe, 1)
            pool.memset(y_sb, 0.0).then_inc(main.ye, 1)

        @block.scalar
        def _(act):
            def store_projection(g):
                b = 2 * (g % 2)
                act.wait_ge(s_wu, UNITS * (g + 1))
                if g < 8:
                    act.activation(A_QK[:, g * 1024:(g + 1) * 1024], bank(b, 2), ACT.Copy).then_inc(s_proje, 1)
                elif g < 11:
                    act.activation(vA[:, :, (g - 8) * HALF:(g - 7) * HALF], ps[:, b:b + 2, :], ACT.Copy).then_inc(s_proje, 1)
                elif g < 13:
                    act.activation(vR[:, :, (g - 11) * HALF:(g - 10) * HALF], ps[:, b:b + 2, :], ACT.Copy).then_inc(s_proje, 1)
                elif g < 15:
                    if g == 13:
                        act.wait_ge(s_pt, SLOTS * GROUPS)
                    act.activation(gr[:, :, (g - 13) * HALF:(g - 12) * HALF], ps[:, b:b + 2, :], ACT.Silu).then_inc(s_proje, 1)
                else:
                    to = (gateA, gateR)[(g - 15) // 2][:, 4 * ((g - 15) % 2):4 * ((g - 15) % 2) + 4, :]
                    act.activation(to.rearrange("p c t -> p (c t)"), bank(b, 2), ACT.Sigmoid).then_inc(s_proje, 1)

            def high(u):
                raw, hi, _ = unit_views(u)
                act.wait_ge(s_win[u // UNITS % W_BUFS][u % UNITS // 2], 16 * (u // UNITS // W_BUFS + 1))
                if u >= UNITS:
                    act.wait_ge(s_wu, u - UNITS + 1)
                act.activation(hi, raw, ACT.Copy).then_inc(s_wh, 1)

            def store_and_split(g):
                for u in range(UNITS - 1):
                    high(UNITS * (g + 1) + u)
                store_projection(g)
                high(UNITS * (g + 1) + UNITS - 1)

            for t in range(TT):
                act.wait_ge(s_x[t], 16)
                if t:
                    act.wait_ge(s_sq, t)
                act.activation(gr[:, 0, :], xb[:, t, :], ACT.Square, accum_out=ssq[:, t:t + 1]).then_inc(s_sq, 1)
            act.wait_ge(s_ms, 1)
            act.activation(rstd, rstd, ACT.Sqrt).then_inc(s_root, 1)
            for b in range(4):
                high(b)
                act.wait_ge(s_ht, b + 1)
                act.activation(hT_hi[:, 2 * b:2 * b + 2, :].rearrange("p c t -> p (c t)"), bank(4 + b), ACT.Copy)\
                    .then_inc(s_hte, 1)
            act.dma_start(gain[:, :], bass.AP(g_ffn.tensor, 0, [[0, P], [1, D]])).then_inc(s_gain, 16)
            store_and_split(0)
            act.dma_start(decay, c_decay.rearrange("p (h i) -> p h i", h=RH)).then_inc(s_decay, 16)
            act.dma_start(wr_sb[:, :, :], w_router.rearrange("(k p) e -> p k e", p=P)).then_inc(s_small, 16)
            act.dma_start(br_sb[:, :], bass.AP(b_router.tensor, 0, [[0, P], [1, N_EXP]])).then_inc(s_small, 16)
            act.dma_start(item_sb[:, :], c_item).then_inc(s_small, 16)
            act.dma_start(expert_sb[:, :], c_expert).then_inc(s_small, 16)
            with nc.allow_non_contiguous_dma(reason="1024 words, off the critical path"):
                act.dma_start(g_col[:, :], g_ffn.rearrange("(k p) -> p k", p=P)).then_inc(s_small, 16)
            for g in range(1, 5):
                store_and_split(g)
            for n in range(6):
                act.wait_ge(s_flip, n + 1)
                act.activation(toep[:, 2 * n:2 * n + 2, :].rearrange("p h c -> p (h c)"), bank(4 + n % 4), ACT.Copy)\
                    .then_inc(s_flipe, 1)

            def exps(s):
                act.wait_ge(s_max, s + 1)
                act.activation(probs[:, s % 2, :, 0:P], probs[:, s % 2, :, 0:P], ACT.Exp,
                               bias=negmax[:, 2 * s:2 * s + 1], accum_out=denom[:, 2 * s:2 * s + 1]).then_inc(s_exp, 1)
                act.activation(probs[:, s % 2, :, P:384], probs[:, s % 2, :, P:384], ACT.Exp,
                               bias=negmax[:, 2 * s + 1:2 * s + 2],
                               accum_out=denom[:, 2 * s + 1:2 * s + 2]).then_inc(s_exp, 1)

            def store_pt(s):
                for g in range(GROUPS):
                    act.wait_ge(s_pt, GROUPS * s + g + 1)
                    if s >= 2:
                        act.wait_ge(s_pv, s - 1)
                    act.activation(ptb[:, s % 2, g, :], ps[:, 4 + g, 0:384], ACT.Copy).then_inc(s_pte, 1)

            for g in range(5, 10):
                store_and_split(g)
            exps(0)
            for s in range(SLOTS):
                store_and_split(10 + s)
                store_pt(s)
                if s + 1 < SLOTS:
                    exps(s + 1)
            store_and_split(14)
            act.wait_ge(s_rv, 1)
            act.activation(rrstd, rrstd, ACT.Sqrt).then_inc(s_rr, 1)
            store_and_split(15)
            store_and_split(16)
            store_and_split(17)
            for b in range(4):
                act.wait_ge(s_rt, b + 1)
                act.activation(retT[:, 2 * b:2 * b + 2, :].rearrange("p c t -> p (c t)"), bank(4 + b), ACT.Copy)\
                    .then_inc(s_rte, 1)
            store_projection(18)

            def high_out(k):
                raw, hi, _ = wout_views(k)
                act.wait_ge(*((s_wouta, 16) if k < 5 else (s_woutb, 16)))
                act.wait_ge(s_wu, LAST_UNIT + k - UNITS + 1)
                act.activation(hi, raw, ACT.Copy).then_inc(s_wh, 1)

            for k in range(UNITS):
                high_out(k)
            for j in range(4):
                act.wait_ge(s_mg, j + 1)
                act.activation(mergedT_hi[:, 2 * j:2 * j + 2, :], mergedT[:, 2 * j:2 * j + 2, :], ACT.Copy)\
                    .then_inc(s_mh, 1)
            for k in range(UNITS, KC):
                high_out(k)
            for t in range(TT):
                act.wait_ge(s_x2, t + 1)
                if t:
                    act.wait_ge(s_sq, TT + t)
                act.activation(junk, xb[:, t, :], ACT.Square, accum_out=ssq[:, t:t + 1]).then_inc(s_sq, 1)
            act.wait_ge(s_ms, 2)
            act.activation(rstd, rstd, ACT.Sqrt).then_inc(s_root, 1)
            for n in range(3):
                for t in range(TT):
                    if n:
                        act.wait_ge(s_rest, TT * (n - 1) + t + 1)
                    else:
                        act.wait_ge(s_h, TT + t + 1)
                    act.activation(xs[:, n, t, :], rest[:, t, :] if n else xn[:, t, :], ACT.Copy).then_inc(s_split, 1)
            for t in range(TT):
                act.wait_ge(s_tk, t + 1)
                act.activation(top[:, t * 64 + 16:t * 64 + 20], top[:, t * 64:t * 64 + 4], ACT.Exp,
                               bias=top[:, t * 64 + 24:t * 64 + 25],
                               accum_out=top[:, t * 64 + 25:t * 64 + 26]).then_inc(s_tke, 1)
            act.wait_ge(s_h, 2 * TT)
            act.dma_start(gain[:, :], bass.AP(g_final.tensor, 0, [[0, P], [1, D]])).then_inc(s_gain, 16)

            def store_x(s, i):
                act.wait_ge(s.gathered, i + 1)
                act.activation(XT.rearrange("p k s -> p (k s)"), bank(6), ACT.Copy).then_inc(s.x, 1)

            def sigmoid(s, i):
                act.wait_ge(s.g, i + 1)
                act.activation(sg, gl, ACT.Sigmoid, scale=ALPHA).then_inc(s.sig, 1)

            def store_act_low(s, i):
                act.wait_ge(s.at, i * 2 + 1)
                act.activation(actT[:, 0:256], ps[:, 6, 0:256], ACT.Copy).then_inc(s.at_lo, 1)

            store_x(main, 0)
            with act.Fori(0, N_EXP) as i:
                sigmoid(main, i)
                store_x(main, i + 1)
                store_act_low(main, i)
            act.wait_ge(s_table, 1)
            n = act.value_load(list_i[0:1, 0:1], min_val=0, max_val=MAX_EXTRA)
            with act.If(n > 0):
                with act.Fori(0, n) as i:
                    store_x(extra, i)
                    sigmoid(extra, i)
                    store_act_low(extra, i)
            for t in range(TT):
                act.wait_ge(s_x2, TT + t + 1)
                if t:
                    act.wait_ge(s_sq, 2 * TT + t)
                act.activation(junk, xb[:, t, :], ACT.Square, accum_out=ssq[:, t:t + 1]).then_inc(s_sq, 1)
            act.wait_ge(s_ms, 3)
            act.activation(rstd, rstd, ACT.Sqrt).then_inc(s_root, 1)

        @block.tensor
        def _(pe):
            def transposes(src, first_bank, done):
                for c in range(KC):
                    for t in range(TT):
                        o = (c % 2) * T + t * P
                        mm = pe.transpose(ps[:, first_bank + c // 2, o:o + P], src[:, t, c * P:(c + 1) * P], ident)
                    if c % 2:
                        mm.then_inc(done, 1)

            pe.wait_ge(s_last, 16)
            pe.wait_ge(s_h, TT)
            transposes(xb, 4, s_ht)

            def turn_bias_tiles():
                pe.wait_ge(s_early, 16)
                pe.wait_ge(s_toep, 16)
                for n in range(6):
                    if n >= 4:
                        pe.wait_ge(s_flipe, n - 3)
                    pe.matmul(bank(4 + n % 4), flip, toep_up[:, n * HALF:(n + 1) * HALF], start=True, stop=True)\
                        .then_inc(s_flip, 1)

            def project(g):
                b = 2 * (g % 2)
                if g >= 2:
                    pe.wait_ge(s_proje, g - 1)
                for u in range(UNITS):
                    pe.wait_ge(s_wl, UNITS * g + u + 1)
                    if g == 0:
                        pe.wait_ge(s_hte, u + 1)
                        pe.wait_ge(s_htl, u + 1)
                    for kk in range(2):
                        k = 2 * u + kk
                        first, last = k == 0, k == KC - 1
                        hi, lo = w_parts[:, u, 0, kk, :], w_parts[:, u, 1, kk, :]
                        if g < 8 or g >= 15:
                            for c in range(4):
                                o = ps[:, b + c // 2, (c % 2) * T:(c % 2 + 1) * T]
                                wh, wl = hi[:, c * P:(c + 1) * P], lo[:, c * P:(c + 1) * P]
                                pe.matmul(o, wh, hT_hi[:, k, :], start=first and c % 2 == 0, stop=False,
                                          skip_group_check=True)
                                pe.matmul(o, wh, hT_lo[:, k, :], start=False, stop=False, skip_group_check=True)
                                mm = pe.matmul(o, wl, hT_hi[:, k, :], start=False, stop=last, skip_group_check=True)
                        else:
                            for t in range(TT):
                                hh, hl = hT_hi[:, k, t * P:(t + 1) * P], hT_lo[:, k, t * P:(t + 1) * P]
                                pe.matmul(bank(b + t), hh, hi, start=first, stop=False)
                                pe.matmul(bank(b + t), hh, lo, start=False, stop=False)
                                mm = pe.matmul(bank(b + t), hl, hi, start=False, stop=last)
                    mm.then_inc(s_wu, 1)

            def rotate_pairs():
                pe.wait_ge(s_early, 16)
                pe.wait_ge(s_proje, 8)
                pe.wait_ge(s_flipe, 6)
                for i in range(2):
                    for h in range(RH):
                        mm = pe.matmul(psf[:, 4 * HALF + (4 * i + h) * T:4 * HALF + (4 * i + h + 1) * T], rot,
                                       qk[:, 6 + i, h, :], start=True, stop=True)
                    mm.then_inc(s_rotm, 1)

            def scores(s):
                if s == 0:
                    pe.wait_ge(s_rotd, 3)
                else:
                    pe.wait_ge(s_pte, GROUPS * s)
                for g in range(GROUPS):
                    pe.matmul(psf[:, 4 * HALF + g * T:4 * HALF + (g + 1) * T], qk[:, g, s, P:T], qk[:, 3 + g, s, :],
                              start=True, stop=True)
                for g in range(GROUPS):
                    mm = pe.matmul(ps[:, 6, g * P:(g + 1) * P], qk[:, g, s, 0:P], qk[:, 3 + g, s, 0:P],
                                   start=True, stop=True)
                mm.then_inc(s_sc, 1)

            def transpose_probs(s):
                pe.wait_ge(s_diag, 2 * (s + 1))
                for g in range(GROUPS):
                    for n, (tile, k) in enumerate(((0, 0), (1, 0), (1, 1))):
                        mm = pe.matmul(ps[:, 4 + g, n * P:(n + 1) * P], probs[:, s % 2, g, (tile + k) * P:(tile + k + 1) * P],
                                       diag[:, 2 * s + tile, :], start=True, stop=True)
                    mm.then_inc(s_pt, 1)

            def attend(s):
                pe.wait_ge(s_pte, GROUPS * (s + 1))
                pe.wait_ge(s_proje, 11)
                if s == SLOTS - 1:
                    pe.wait_ge(s_rse, RH)
                elif s:
                    pe.wait_ge(s_pve, s)
                for g in range(GROUPS):
                    c = (g * SLOTS + s) * P
                    pe.matmul(ps[:, 7, 0:T], vA[:, 0, c:c + P], ptb[:, s % 2, g, 0:T],
                              start=(g == 0), stop=False)
                    mm = pe.matmul(ps[:, 7, P:T], vA[:, 1, c:c + P], ptb[:, s % 2, g, T:384],
                                   start=False, stop=(g == GROUPS - 1))
                mm.then_inc(s_pv, 1)

            def ret_scores():
                pe.wait_ge(s_rotd, 4)
                pe.wait_ge(s_pte, GROUPS * SLOTS)
                for h in range(RH):
                    if h == 3:
                        pe.wait_ge(s_pve, 3)
                    pe.matmul(ps[:, 4 + h, 0:T], qk[:, 7, h, 0:P], qk[:, 6, h, :], start=True, stop=True)
                    pe.matmul(ps[:, 4 + h, T:384], qk[:, 7, h, P:T], qk[:, 6, h, P:T], start=True, stop=True)\
                        .then_inc(s_rs, 1)

            def ret_out():
                pe.wait_ge(s_rse, RH)
                pe.wait_ge(s_proje, 13)
                for t in range(TT):
                    if t == 1:
                        pe.wait_ge(s_pve, 4)
                    for h in range(RH):
                        o = psf[:, (4 + 2 * t) * HALF + h * DV:(4 + 2 * t) * HALF + (h + 1) * DV]
                        mm = pe.matmul(o, st[:, h, t * P:(t + 1) * P], vR[:, 0, h * DV:(h + 1) * DV],
                                       start=True, stop=(t == 0))
                        if t == 1:
                            mm = pe.matmul(o, st[:, h, T:384], vR[:, 1, h * DV:(h + 1) * DV], start=False, stop=True)
                    mm.then_inc(s_ro, 1)

            project(0)
            pe.wait_ge(s_biasin, 48)
            pe.matmul(ps[0:N_ATT_HEADS, 7, 0:384], rel_sb, onehot_sb, start=True, stop=True).then_inc(s_tabp, 1)
            for g in range(1, 5):
                project(g)
            turn_bias_tiles()
            for g in range(5, 9):
                project(g)
            rotate_pairs()
            project(9)
            scores(0)
            for s in range(SLOTS):
                project(10 + s)
                transpose_probs(s)
                if s >= 1:
                    attend(s - 1)
                if s + 1 < SLOTS:
                    scores(s + 1)
            ret_scores()
            project(14)
            attend(SLOTS - 1)
            ret_out()
            project(15)
            project(16)
            project(17)
            pe.wait_ge(s_rg, 2)
            transposes(gr, 4, s_rt)
            project(18)
            pe.wait_ge(s_watt, 16)
            pe.wait_ge(s_pve, SLOTS)
            pe.wait_ge(s_wret, 32)
            pe.wait_ge(s_rte, 4)
            for j in range(4):
                b = 2 * ((j + 1) % 2)
                if j < 2:
                    pe.wait_ge(s_proje, 18 + j)
                else:
                    pe.wait_ge(s_mg, j - 1)
                for i in range(2):
                    c = 2 * j + i
                    for k in range(4):
                        pe.matmul(ps[:, b, i * T:(i + 1) * T], watt[:, k, c * P:(c + 1) * P], attT[:, k, :],
                                  start=(k == 0), stop=(k == 3))
                for i in range(2):
                    c = 2 * j + i
                    for k in range(KC):
                        mm = pe.matmul(ps[:, b + 1, i * T:(i + 1) * T], wret[:, k, c * P:(c + 1) * P], retT[:, k, :],
                                       start=(k == 0), stop=(k == KC - 1))
                mm.then_inc(s_br, 1)
            for k in range(KC):
                pe.wait_ge(s_ml, k // 2 + 1)
                pe.wait_ge(s_wl, LAST_UNIT + k + 1)
                for t in range(TT):
                    mh, ml = mergedT_hi[:, k, t * P:(t + 1) * P], mergedT_lo[:, k, t * P:(t + 1) * P]
                    for half in range(2):
                        o = bank(4 + 2 * t + half)
                        wh, wl = w_parts[:, k % UNITS, 0, half, :], w_parts[:, k % UNITS, 1, half, :]
                        pe.matmul(o, mh, wh, start=(k == 0), stop=False)
                        pe.matmul(o, mh, wl, start=False, stop=False)
                        mm = pe.matmul(o, ml, wh, start=False, stop=(k == KC - 1))
                    if k == KC - 1:
                        mm.then_inc(s_wo, 1)
                if k < KC - UNITS:
                    mm.then_inc(s_wu, 1)
            pe.wait_ge(s_x2, TT)
            transposes(xb, 0, s_xt)
            pe.wait_ge(s_wr, KC)
            pe.wait_ge(s_xte, 4)
            for t in range(TT):
                for k in range(KC):
                    mm = pe.matmul(ps[:, 4, t * N_EXP:(t + 1) * N_EXP], xT[:, k, t * P:(t + 1) * P], wr_sb[:, k, :],
                                   start=(k == 0), stop=(k == KC - 1))
            mm.then_inc(s_lg, 1)
            pe.wait_ge(s_bf, 3)
            pe.wait_ge(s_mask, TT)
            pe.matmul(ps[:, 5, 0:32], before_bf[:, :], mask_bf[:, 0, :], start=True, stop=True)
            pe.matmul(ps[:, 5, 32:64], before_bf[:, :], mask_bf[:, 1, :], start=True, stop=False)
            pe.matmul(ps[:, 5, 32:64], ones_bf[:, :], mask_bf[:, 0, :], start=False, stop=True)
            pe.matmul(ps[:, 5, 64:96], ones_bf[:, :], mask_bf[:, 0, :], start=True, stop=False)
            pe.matmul(ps[:, 5, 64:96], ones_bf[:, :], mask_bf[:, 1, :], start=False, stop=True).then_inc(s_pos, 1)

            def gather(s, i):
                pe.wait_ge(s.slots, i + 1)
                for k in range(KC):
                    for part in range(3):
                        for t in range(TT):
                            mm = pe.matmul(ps[:, 6, k * CAP:(k + 1) * CAP], xs[:, part, t, k * P:(k + 1) * P],
                                           s_one[:, t, :], start=(part == 0 and t == 0), stop=(part == 2 and t == 1))
                mm.then_inc(s.gathered, 1)

            def hidden(s, i):
                pe.wait_ge(s.b1, i * 16 + 16)
                pe.wait_ge(s.x, i + 1)
                for c in range(4):
                    o = ps[CAP * (c % 2):CAP * (c % 2) + CAP, 4 + c // 2, :]
                    mm = pe.matmul(o, first_row, b1_row[:, c * HALF:(c + 1) * HALF], start=True, stop=False)
                mm.then_inc(s.b1_used, 1)
                for k in range(KC):
                    pe.wait_ge(s.w1[k], i * 16 + 16)
                    for c in range(4):
                        o = ps[CAP * (c % 2):CAP * (c % 2) + CAP, 4 + c // 2, :]
                        mm = pe.matmul(o, XT[:, k, :], w1_ring[:, k, c * HALF:(c + 1) * HALF],
                                       start=False, stop=(k == KC - 1))
                    mm.then_inc(s.w1_used, 1)

            def transpose_act(s, i):
                pe.wait_ge(s.act, i + 1)
                for j in range(4):
                    mm = pe.transpose(ps[:, 6 + j // 2, (j % 2) * P:(j % 2 + 1) * P], act_sb[:, j * P:(j + 1) * P], ident)
                    if j % 2:
                        mm.then_inc(s.at, 1)

            def project_down(s, i):
                pe.wait_ge(s.at_lo, i + 1)
                pe.wait_ge(s.at_hi, i + 1)
                pe.wait_ge(s.b2, i * 16 + 16)
                for c in range(2):
                    pe.matmul(ps[CAP * c:CAP * c + CAP, 7, :], first_row, b2_row[:, c * HALF:(c + 1) * HALF],
                              start=True, stop=False)
                for n, q in enumerate((0, 1, 2, 3, 4, 5, 6, 7)):
                    if q % 2 == 0:
                        pe.wait_ge(s.w2[q // 2], i * 16 + 16)
                    for c in range(2):
                        lhs = actT[:, (q % 4) * P + (q // 4) * CAP:(q % 4) * P + (q // 4) * CAP + CAP]
                        mm = pe.matmul(ps[CAP * c:CAP * c + CAP, 7, :], lhs, w2_ring[:, q, c * HALF:(c + 1) * HALF],
                                       start=False, stop=(n == FQ - 1))
                    if q % 2:
                        mm.then_inc(s.w2_used, 1)

            def transpose_slots(s, i):
                pe.wait_ge(s.wslots, i + 1)
                pe.wait_ge(s.at_lo, i + 1)
                for t in range(TT):
                    mm = pe.transpose(ps[:, 6, t * P:(t + 1) * P], s_w[:, t, :], ident)
                mm.then_inc(s.sw, 1)

            def scatter(s, i):
                pe.wait_ge(s.ye, i + 1)
                pe.wait_ge(s.swe, i + 1)
                for t in range(TT):
                    for c in range(2):
                        mm = pe.matmul(bank(2 * t + c), sc_w[:, c, t * P:(t + 1) * P], y_sb, start=False, stop=True,
                                       skip_group_check=True)
                mm.then_inc(s_scattered, 1)

            pe.wait_ge(s_split, 3 * TT)
            gather(main, 0)
            for b in range(4):
                pe.matmul(bank(b), ones_bf[:, :], zeros_bf[:, :], start=True, stop=True)
            with pe.Fori(0, N_EXP) as i:
                hidden(main, i)
                pe.wait_ge(main.swe, i + 1)
                gather(main, i + 1)
                scatter(main, i)
                pe.wait_ge(main.x, i + 2)
                transpose_act(main, i)
                project_down(main, i)
                transpose_slots(main, i)
            scatter(main, N_EXP)
            pe.wait_ge(s_table, 1)
            n = pe.value_load(list_i[0:1, 0:1], min_val=0, max_val=MAX_EXTRA)
            with pe.If(n > 0):
                with pe.Fori(0, n) as i:
                    gather(extra, i)
                    hidden(extra, i)
                    transpose_act(extra, i)
                    project_down(extra, i)
                    transpose_slots(extra, i)
                    scatter(extra, i)

        @block.vector
        def _(dve):
            chain = [0]

            def link(ins):
                chain[0] += 1
                ins.then_inc(s_dve, 1)
                dve.wait_ge(s_dve, chain[0])

            def root_mean_square(n):
                dve.wait_ge(s_sq, n * TT)
                dve.tensor_scalar(rstd, ssq, 1.0 / D, EPS, ALU.mult, ALU.add).then_inc(s_ms, 1)
                dve.wait_ge(s_root, n)
                link(dve.reciprocal(rstd, rstd))

            def low(u):
                raw, hi, lo = unit_views(u)
                dve.wait_ge(s_wh, u + 1)
                dve.tensor_tensor(lo, raw, hi.bitcast(F32), ALU.subtract).then_inc(s_wl, 1)

            root_mean_square(1)
            dve.wait_ge(s_gain, 16)
            for t in range(TT):
                dve.scalar_tensor_tensor(xb[:, t, :], xb[:, t, :], rstd[:, t:t + 1], gain[:, :],
                                         ALU.mult, ALU.mult).then_inc(s_h, 1)
            dve.wait_ge(s_ht, 4)
            for b in range(4):
                low(b)
                dve.wait_ge(s_hte, b + 1)
                h2 = slice(2 * b, 2 * b + 2)
                dve.tensor_tensor(hT_lo[:, h2, :].rearrange("p c t -> p (c t)"), bank(4 + b),
                                  hT_hi[:, h2, :].rearrange("p c t -> p (c t)").bitcast(F32), ALU.subtract)\
                    .then_inc(s_htl, 1)

            for u in range(3):
                low(UNITS + u)
            dve.wait_ge(s_tabp, 1)
            dve.tensor_tensor(tab_sb, ps[0:N_ATT_HEADS, 7, 0:384], mask_sb, ALU.add).then_inc(s_tabd, 1)
            low(UNITS + 3)
            for u in range(2 * UNITS, 3 * UNITS):
                low(u)
            dve.wait_ge(s_small, 80)
            for k in range(KC):
                dve.tensor_scalar(wr_sb[:, k, :], wr_sb[:, k, :], g_col[:, k:k + 1], None, ALU.mult).then_inc(s_wr, 1)
            for u in range(3 * UNITS, 10 * UNITS):
                low(u)

            cos4 = cosT.rearrange("p (a t) -> p a t", a=1).broadcast_to([P, 4, T])
            sin4 = sinT.rearrange("p (a t) -> p a t", a=1).broadcast_to([P, 4, T])
            rt4 = rtmp.rearrange("p (a t) -> p a t", a=4)
            for i in range(2):
                dve.wait_ge(s_rotm, i + 1)
                dve.tensor_tensor(rt4, bank(4 + 2 * i, 2).rearrange("p (a t) -> p a t", a=4), sin4, ALU.mult)\
                    .then_inc(s_rotd, 1)
                link(dve.tensor_tensor(qk[:, 6 + i, :, :], qk[:, 6 + i, :, :], cos4, ALU.mult))
                dve.wait_ge(s_rotd, 2 * i + 1)
                dve.tensor_tensor(qk[:, 6 + i, :, :], qk[:, 6 + i, :, :], rt4, ALU.add).then_inc(s_rotd, 1)
                dve.wait_ge(s_rotd, 2 * i + 2)
                low(10 * UNITS + i)
            for u in range(2, UNITS):
                low(10 * UNITS + u)

            dve.wait_ge(s_flipe, 6)

            def store_scores(s):
                dve.wait_ge(s_sc, s + 1)
                if s >= 2:
                    dve.wait_ge(s_pt, GROUPS * (s - 1))
                p3 = psf[:, 4 * HALF:4 * HALF + GROUPS * T].rearrange("p (g k) -> p g k", g=GROUPS)
                p2 = ps[:, 6, 0:GROUPS * P].rearrange("p (g k) -> p g k", g=GROUPS)
                heads = toep[:, s:N_ATT_HEADS:SLOTS, :]
                b = s % 2
                dve.scalar_tensor_tensor(probs[:, b, :, P:384], p3, ATT_SCALE, heads, ALU.mult, ALU.add)
                link(dve.scalar_tensor_tensor(probs[:, b, :, 0:P], p2, ATT_SCALE, heads[:, :, P:T], ALU.mult, ALU.add))
                dve.tensor_reduce(maxes[:, 2 * s:2 * s + 1], probs[:, b, :, 0:P], AX.XY, ALU.max)
                link(dve.tensor_reduce(maxes[:, 2 * s + 1:2 * s + 2], probs[:, b, :, P:384], AX.XY, ALU.max))
                dve.tensor_scalar(negmax[:, 2 * s:2 * s + 2], maxes[:, 2 * s:2 * s + 2], -1.0, None, ALU.mult)\
                    .then_inc(s_max, 1)

            def softmax_scales(s):
                dve.wait_ge(s_exp, 2 * s + 2)
                link(dve.reciprocal(rden[:, 2 * s:2 * s + 2], denom[:, 2 * s:2 * s + 2]))
                for t in range(TT):
                    dve.tensor_scalar(diag[:, 2 * s + t, :], ident, rden[:, 2 * s + t:2 * s + t + 1], None, ALU.mult)\
                        .then_inc(s_diag, 1)

            def store_att(s):
                dve.wait_ge(s_pv, s + 1)
                dve.tensor_copy(attT[:, s, :], ps[:, 7, 0:T]).then_inc(s_pve, 1)

            dve.wait_ge(s_last, 16)
            for s in range(SLOTS):
                if s >= 2:
                    store_att(s - 2)
                store_scores(s)
                softmax_scales(s)
                for u in range(UNITS):
                    low((11 + s) * UNITS + u)
            store_att(2)
            dve.wait_ge(s_decay, 16)
            for h in range(RH):
                dve.wait_ge(s_rs, h + 1)
                dve.tensor_tensor(st[:, h, 0:T], ps[:, 4 + h, 0:T], decay[:, h, :], ALU.mult)
                dve.tensor_tensor(st[:, h, T:384], ps[:, 4 + h, T:384], decay[:, h, 0:P], ALU.mult).then_inc(s_rse, 1)
            for u in range(UNITS):
                low(15 * UNITS + u)
            store_att(3)

            def ret_head(t, h):
                return psf[:, (4 + 2 * t) * HALF + h * DV:(4 + 2 * t) * HALF + (h + 1) * DV]

            for t in range(TT):
                dve.wait_ge(s_ro, t + 1)
                for h in range(RH):
                    last = dve.bn_stats(bns[:, 4 * t + h, :], ret_head(t, h))
            link(last)
            for n in range(8):
                last = dve.bn_aggr(mv[:, n, :], bns[:, n, :])
            link(last)
            dve.tensor_scalar(rrstd, mv[:, :, 1], EPS, None, ALU.add).then_inc(s_rv, 1)
            low(16 * UNITS)
            low(16 * UNITS + 1)
            dve.wait_ge(s_rr, 1)
            link(dve.reciprocal(rrstd, rrstd))
            dve.wait_ge(s_proje, 15)
            for t in range(TT):
                for h in range(RH):
                    n = 4 * t + h
                    last = dve.tensor_scalar(gr[:, t, h * DV:(h + 1) * DV], gr[:, t, h * DV:(h + 1) * DV],
                                             rrstd[:, n:n + 1], None, ALU.mult)
                link(last)
                for h in range(RH):
                    n = 4 * t + h
                    last = dve.scalar_tensor_tensor(gr[:, t, h * DV:(h + 1) * DV], ret_head(t, h), mv[:, n, 0:1],
                                                    gr[:, t, h * DV:(h + 1) * DV], ALU.subtract, ALU.mult)
                last.then_inc(s_rg, 1)
                for u in range(2):
                    low(16 * UNITS + 2 + 2 * t + u)
            for u in range(17 * UNITS + 2, LAST_UNIT):
                low(u)

            def low_out(k):
                raw, hi, lo = wout_views(k)
                dve.wait_ge(s_wh, LAST_UNIT + k + 1)
                dve.tensor_tensor(lo, raw, hi.bitcast(F32), ALU.subtract).then_inc(s_wl, 1)

            for k in range(UNITS):
                low_out(k)
            for j in range(4):
                dve.wait_ge(s_br, j + 1)
                dve.wait_ge(s_proje, 18 + j // 2)
                b = 2 * ((j + 1) % 2)
                mg = mergedT[:, 2 * j:2 * j + 2, :].rearrange("p c t -> p (c t)")
                ga = gateA[:, 2 * j:2 * j + 2, :].rearrange("p c t -> p (c t)")
                gg = gateR[:, 2 * j:2 * j + 2, :].rearrange("p c t -> p (c t)")
                dve.tensor_tensor(mg, bank(b), ga, ALU.mult)
                link(dve.tensor_tensor(gg, bank(b + 1), gg, ALU.mult))
                dve.tensor_tensor(mg, mg, gg, ALU.add).then_inc(s_mg, 1)
                dve.wait_ge(s_mh, j + 1)
                dve.tensor_tensor(mergedT_lo[:, 2 * j:2 * j + 2, :], mergedT[:, 2 * j:2 * j + 2, :],
                                  mergedT_hi[:, 2 * j:2 * j + 2, :].bitcast(F32), ALU.subtract).then_inc(s_ml, 1)
            for k in range(UNITS, KC):
                low_out(k)
            for t in range(TT):
                dve.wait_ge(s_x[t], 32)
                dve.wait_ge(s_wo, t + 1)
                dve.tensor_tensor(xb[:, t, :], xb[:, t, :], bank(4 + 2 * t, 2), ALU.add).then_inc(s_x2, 1)
            for b in range(4):
                dve.wait_ge(s_xt, b + 1)
                dve.tensor_copy(xT[:, 2 * b:2 * b + 2, :].rearrange("p c t -> p (c t)"), bank(b)).then_inc(s_xte, 1)
            root_mean_square(2)
            dve.wait_ge(s_gain, 32)
            for t in range(TT):
                dve.scalar_tensor_tensor(xn[:, t, :], xb[:, t, :], rstd[:, t:t + 1], gain[:, :],
                                         ALU.mult, ALU.mult).then_inc(s_h, 1)
            for n in range(2):
                for t in range(TT):
                    dve.wait_ge(s_split, TT * n + t + 1)
                    dve.tensor_tensor(rest[:, t, :], rest[:, t, :] if n else xn[:, t, :], xs[:, n, t, :], ALU.subtract)\
                        .then_inc(s_rest, 1)
            dve.wait_ge(s_lg, 1)
            lg = [top[:, t * 64 + 32:t * 64 + 64] for t in range(TT)]
            for t in range(TT):
                last = dve.scalar_tensor_tensor(lg[t], ps[:, 4, t * N_EXP:(t + 1) * N_EXP], rstd[:, t:t + 1],
                                                br_sb[:, :], ALU.mult, ALU.add)
            link(last)
            for t in range(TT):
                last = dve.max(top[:, t * 64:t * 64 + 8], lg[t])
            link(last)
            for t in range(TT):
                dve.tensor_scalar(top[:, t * 64 + 24:t * 64 + 25], top[:, t * 64:t * 64 + 1], -1.0, None, ALU.mult)\
                    .then_inc(s_tk, 1)
                last = dve.max_index(top[:, t * 64 + 8:t * 64 + 16].bitcast(U32), top[:, t * 64:t * 64 + 8], lg[t])
            link(last)
            chosen = A_W[:, 4096:4096 + 2 * TT * TOP_K * N_EXP].rearrange("p (m t j e) -> p m t j e", m=2, t=TT, j=TOP_K)
            for t in range(TT):
                last = dve.tensor_copy(top[:, t * 64 + 20:t * 64 + 24], top[:, t * 64 + 8:t * 64 + 12].bitcast(U32))
            link(last)
            for t in range(TT):
                for j in range(TOP_K):
                    last = dve.tensor_scalar(chosen[:, 0, t, j, :], expert_sb[:, :], top[:, t * 64 + 20 + j:t * 64 + 21 + j],
                                             None, ALU.is_equal)
            link(last)
            for t in range(TT):
                last = dve.tensor_reduce(mask_f[:, t, :], chosen[:, 0, t, :, :].rearrange("p j e -> p e j"), AX.X, ALU.add)
            link(last)
            for t in range(TT):
                dve.tensor_copy(mask_bf[:, t, :], mask_f[:, t, :]).then_inc(s_mask, 1)
            dve.wait_ge(s_pos, 1)
            for t in range(TT):
                last = dve.scalar_tensor_tensor(posm[:, t, 3 * N_EXP:], ps[:, 5, t * 32:(t + 1) * 32], 1.0,
                                                mask_f[:, t, :], ALU.add, ALU.mult)
            link(last)
            for b in range(4):
                last = dve.tensor_scalar(posm[:, :, b * N_EXP:(b + 1) * N_EXP], posm[:, :, 3 * N_EXP:], -1.0 - b * CAP,
                                         None, ALU.add)
            link(last)

            def slots(s, i, col):
                for t in range(TT):
                    last = dve.tensor_scalar(s_one[:, t, :], slot_ids[:, 0:CAP], posm[:, t, bass.ds(col, 1)], None,
                                             ALU.is_equal)
                last.then_inc(s.slots, 1)

            dve.tensor_scalar(lists[0:1, 96:128], ps[0:1, 5, 64:96], 0.0, None, ALU.add)
            slots(main, 0, 0)
            dve.wait_ge(s_tke, TT)
            for t in range(TT):
                last = dve.reciprocal(top[:, t * 64 + 26:t * 64 + 27], top[:, t * 64 + 25:t * 64 + 26])
            link(last)
            for t in range(TT):
                last = dve.tensor_scalar(top[:, t * 64 + 16:t * 64 + 20], top[:, t * 64 + 16:t * 64 + 20],
                                         top[:, t * 64 + 26:t * 64 + 27], None, ALU.mult)
            link(last)
            for t in range(TT):
                for j in range(TOP_K):
                    last = dve.tensor_scalar(chosen[:, 1, t, j, :], expert_sb[:, :], top[:, t * 64 + 20 + j:t * 64 + 21 + j],
                                             top[:, t * 64 + 16 + j:t * 64 + 17 + j], ALU.is_equal, ALU.mult)
            link(last)
            for t in range(TT):
                last = dve.tensor_reduce(gates[:, t, 0:N_EXP], chosen[:, 1, t, :, :].rearrange("p j e -> p e j"), AX.X,
                                         ALU.add)
            link(last)
            for b in range(1, 4):
                dve.tensor_copy(gates[:, :, b * N_EXP:(b + 1) * N_EXP], gates[:, :, 0:N_EXP])
            keys = top[0:1, 0:128]
            for b in range(4):
                last = dve.tensor_scalar(keys[:, b * N_EXP:(b + 1) * N_EXP], lists[0:1, 96:128],
                                         float(b * CAP) if b else 1.0e9, None, ALU.is_gt)
            link(last)
            link(dve.tensor_reduce(lists[0:1, 64:65], keys, AX.X, ALU.add))
            link(dve.tensor_copy(list_i[0:1, 0:1], lists[0:1, 64:65]))
            link(dve.tensor_tensor(keys, keys, item_sb[:, :], ALU.mult))
            link(dve.max(lists[0:1, 64:72], keys))
            link(dve.match_replace(keys, lists[0:1, 64:72], keys, 0.0))
            link(dve.max(lists[0:1, 72:80], keys))
            link(dve.tensor_scalar(lists[0:1, 64:80], lists[0:1, 64:80], -1.0, float(P), ALU.mult, ALU.add))
            link(dve.tensor_scalar(lists[0:1, 64:80], lists[0:1, 64:80], float(P - 1), None, ALU.min))
            dve.tensor_copy(list_i[0:1, 16:32], lists[0:1, 64:80])
            for b in range(1, 4):
                last = dve.tensor_scalar(lists[0:1, 80:96] if b == 1 else lists[0:1, 96 + 16 * (b - 2):112 + 16 * (b - 2)],
                                         lists[0:1, 64:80], float(b * N_EXP), -float(N_EXP), ALU.is_ge, ALU.mult)
            link(last)
            for b in range(3):
                link(dve.tensor_tensor(lists[0:1, 64:80], lists[0:1, 64:80], lists[0:1, 80 + 16 * b:96 + 16 * b], ALU.add))
            dve.tensor_copy(list_i[0:1, 32:48], lists[0:1, 64:80]).then_inc(s_table, 1)
            dve.wait_ge(s_table, 1)

            def gated_slots(s, i, col):
                for t in range(TT):
                    last = dve.tensor_scalar(s_w[:, t, :], slot_ids, posm[:, t, bass.ds(col, 1)],
                                             gates[:, t, bass.ds(col, 1)], ALU.is_equal, ALU.mult)
                last.then_inc(s.wslots, 1)

            def activate(s, i):
                dve.wait_ge(s.w1_used, i * KC + KC)
                dve.tensor_scalar(gl, bank(4), LIMIT, None, ALU.min).then_inc(s.g, 1)
                dve.tensor_scalar(ul, bank(5), LIMIT, -LIMIT, ALU.min, ALU.max).then_inc(s.chain, 1)
                dve.wait_ge(s.chain, i * 2 + 1)
                dve.wait_ge(s.g, i + 1)
                dve.scalar_tensor_tensor(ul, ul, 1.0, gl, ALU.add, ALU.mult).then_inc(s.chain, 1)
                dve.wait_ge(s.chain, i * 2 + 2)
                dve.wait_ge(s.sig, i + 1)
                dve.tensor_tensor(act_sb, ul, sg, ALU.mult).then_inc(s.act, 1)

            def store_act_high(s, i):
                dve.wait_ge(s.at, i * 2 + 2)
                dve.tensor_copy(actT[:, 256:512], ps[:, 7, 0:256]).then_inc(s.at_hi, 1)

            def store_y(s, i):
                dve.wait_ge(s.w2_used, i * (FQ // 2) + FQ // 2)
                dve.tensor_copy(y_sb, bank(7)).then_inc(s.ye, 1)

            def store_scatter(s, i):
                dve.wait_ge(s.sw, i + 1)
                dve.tensor_copy(sc_w[0:CAP, 0, :], ps[0:CAP, 6, 0:T])
                dve.tensor_copy(sc_w[CAP:P, 1, :], ps[CAP:P, 6, 0:T]).then_inc(s.swe, 1)

            with dve.Fori(0, N_EXP) as i:
                dve.wait_ge(main.gathered, i + 1)
                slots(main, i + 1, i + 1)
                gated_slots(main, i, i)
                activate(main, i)
                store_act_high(main, i)
                store_y(main, i)
                store_scatter(main, i)
            dve.wait_ge(s_scattered, N_EXP + 1)
            n = dve.value_load(list_i[0:1, 0:1], min_val=0, max_val=MAX_EXTRA)
            with dve.If(n > 0):
                with dve.Fori(0, n) as i:
                    item = dve.value_load(list_i[0:1, bass.ds(i + 16, 1)], min_val=0, max_val=P - 1)
                    slots(extra, i, item)
                    gated_slots(extra, i, item)
                    activate(extra, i)
                    store_act_high(extra, i)
                    store_y(extra, i)
                    store_scatter(extra, i)
                dve.wait_ge(s_scattered, n + N_EXP + 1)
                dve.memset(lists[0:1, 64:65], 0.0)
            for t in range(TT):
                dve.tensor_tensor(xb[:, t, :], xb[:, t, :], bank(2 * t, 2), ALU.add).then_inc(s_x2, 1)
            root_mean_square(3)
            dve.wait_ge(s_gain, 48)
            for t in range(TT):
                dve.scalar_tensor_tensor(xb[:, t, :], xb[:, t, :], rstd[:, t:t + 1], gain[:, :],
                                         ALU.mult, ALU.mult).then_inc(s_fin, 1)


_INS = ["x", "norm_mix_g", "w_in", "rel_bias", "w_att_branch", "w_ret_branch", "w_out", "norm_ffn_g",
        "w_router", "b_router", "w1", "b1", "w2", "b2", "norm_final_g"]


def kernel(**inputs):
    import numpy as _np
    import concourse.bacc as _bacc
    from concourse import mybir as _mybir
    from concourse.bass_utils import run_bass_kernel_spmd as _run

    nc = _bacc.Bacc("TRN2", target_bir_lowering=False, num_devices=1)
    arrays, args = {}, []

    def declare(name, a):
        arrays[name] = a
        args.append(nc.dram_tensor(name, a.shape, _mybir.dt.from_np(a.dtype), kind="ExternalInput").ap())

    for name in _INS:
        a = _np.asarray(inputs[name])
        if name not in ("rel_bias", "norm_final_g"):
            a = a[0]
        declare(f"in_{name}", _np.ascontiguousarray(a))
    for name, a in host_constants().items():
        declare(name, _np.ascontiguousarray(a))
    args.append(nc.dram_tensor("out_0", (T, D), F32, kind="ExternalOutput").ap())
    hybrid_block_kernel(nc, *args)
    r = _run(nc, [arrays], core_ids=[0])
    return _np.asarray(r.results[0]["out_0"]).reshape(1, T, D)
```
